# Optimizing a Trainium2 kernel written in Bass

```python
import math
import jax, jax.numpy as jnp
from jax import lax
import numpy as np

D_MODEL = 1024
BATCH = 1
SEQ = 1024
DEPTH = 4

N_MIXERS = 3
BLOCK_Q = 128
EPS = 1e-6

GLA_HEADS = 4
GLA_KEY_DIM = D_MODEL // 2
GLA_VAL_DIM = D_MODEL
GLA_DK = GLA_KEY_DIM // GLA_HEADS
GLA_DV = GLA_VAL_DIM // GLA_HEADS
GLA_GATE_RANK = 16
GLA_GATE_NORMALIZER = 16.0
GLA_CHUNK = 64
GLA_IN = 2 * GLA_KEY_DIM + 2 * GLA_VAL_DIM + GLA_GATE_RANK

MLA_HEADS = 16
MLA_Q_RANK = 256
MLA_KV_RANK = 128
MLA_NOPE = 128
MLA_ROPE = 64
MLA_V = 128
MLA_WIDTH = MLA_HEADS * MLA_V
MLA_IN = MLA_Q_RANK + MLA_KV_RANK + MLA_ROPE + MLA_WIDTH
ROPE_THETA = 10000.0

SB_HEADS = 16
SB_HEAD_DIM = 64
SB_WIDTH = SB_HEADS * SB_HEAD_DIM
SB_IN = 4 * SB_WIDTH

N_GLA_LAYERS = (DEPTH + 2) // 3
N_MLA_LAYERS = (DEPTH + 1) // 3
N_SB_LAYERS = DEPTH // 3

kernel_name = "interleaved_gla_mla_stickbreaking_trunk"

def rmsnorm(x, g):
    xf = x.astype(jnp.float32)
    y = xf * lax.rsqrt(jnp.mean(xf * xf, axis=-1, keepdims=True) + EPS)
    return (y * g.astype(jnp.float32)).astype(x.dtype)

def rope_tables(seq, dim):
    pos = jnp.arange(seq, dtype=jnp.float32)
    inv = ROPE_THETA ** (-jnp.arange(0, dim, 2, dtype=jnp.float32) / dim)
    ang = pos[:, None] * inv[None, :]
    return jnp.cos(ang), jnp.sin(ang)

def apply_rope(x, cos, sin):
    x1, x2 = jnp.split(x, 2, axis=-1)
    c = cos.astype(x.dtype)
    s = sin.astype(x.dtype)
    return jnp.concatenate([x1 * c - x2 * s, x1 * s + x2 * c], axis=-1)

def gla_mixer(h, w_in, w_gate2, b_gate, norm_g, w_out):
    B, S, _ = h.shape
    proj = h @ w_in
    K, V = GLA_KEY_DIM, GLA_VAL_DIM
    q, k, v, g, a_low = jnp.split(proj, [K, 2 * K, 2 * K + V, 2 * K + 2 * V], axis=-1)
    log_a = jax.nn.log_sigmoid((a_low @ w_gate2 + b_gate).astype(jnp.float32)) / GLA_GATE_NORMALIZER
    q = q * (GLA_DK ** -0.5)
    n_chunks = S // GLA_CHUNK

    def to_chunks(t, d):
        return t.astype(jnp.float32).reshape(B, n_chunks, GLA_CHUNK, GLA_HEADS, d).transpose(1, 0, 3, 2, 4)

    qc, kc, vc = to_chunks(q, GLA_DK), to_chunks(k, GLA_DK), to_chunks(v, GLA_DV)
    lac = to_chunks(log_a, GLA_DK)
    mask = jnp.tril(jnp.ones((GLA_CHUNK, GLA_CHUNK), dtype=bool))

    def step(state, inp):
        qb, kb, vb, la = inp
        b = jnp.cumsum(la, axis=2)
        b_last = b[:, :, -1, :]
        o_inter = jnp.einsum('bhtd,bhde->bhte', qb * jnp.exp(b), state)
        diff = b[:, :, :, None, :] - b[:, :, None, :, :]
        decay = jnp.exp(jnp.where(mask[:, :, None], diff, -jnp.inf))
        attn = jnp.einsum('bhtd,bhsd,bhtsd->bhts', qb, kb, decay)
        o_intra = jnp.einsum('bhts,bhse->bhte', attn, vb)
        k_dec = kb * jnp.exp(b_last[:, :, None, :] - b)
        new_state = jnp.exp(b_last)[..., None] * state + jnp.einsum('bhsd,bhse->bhde', k_dec, vb)
        return new_state, o_inter + o_intra

    state0 = jnp.zeros((B, GLA_HEADS, GLA_DK, GLA_DV), jnp.float32)
    _, o = lax.scan(step, state0, (qc, kc, vc, lac))
    o = o.transpose(1, 0, 3, 2, 4).reshape(B, S, GLA_HEADS, GLA_DV).astype(h.dtype)
    o = rmsnorm(o, norm_g).reshape(B, S, GLA_VAL_DIM)
    return (o * jax.nn.silu(g)) @ w_out

def mla_mixer(h, w_in, q_norm_g, kv_norm_g, w_uq, w_ukv, w_out, cos, sin):
    B, S, _ = h.shape
    proj = h @ w_in
    c_q, c_kv, k_rope, g = jnp.split(
        proj, [MLA_Q_RANK, MLA_Q_RANK + MLA_KV_RANK, MLA_Q_RANK + MLA_KV_RANK + MLA_ROPE], axis=-1)
    q = (rmsnorm(c_q, q_norm_g) @ w_uq).reshape(B, S, MLA_HEADS, MLA_NOPE + MLA_ROPE)
    q_nope, q_rope = jnp.split(q, [MLA_NOPE], axis=-1)
    q_rope = apply_rope(q_rope, cos[:, None, :], sin[:, None, :])
    kv = (rmsnorm(c_kv, kv_norm_g) @ w_ukv).reshape(B, S, MLA_HEADS, MLA_NOPE + MLA_V)
    k_nope, v = jnp.split(kv, [MLA_NOPE], axis=-1)
    k_rope = apply_rope(k_rope, cos, sin)
    scale = (MLA_NOPE + MLA_ROPE) ** -0.5
    outs = []
    for i in range(S // BLOCK_Q):
        q0, k_end = i * BLOCK_Q, (i + 1) * BLOCK_Q
        s = (jnp.einsum('bqhd,bkhd->bhqk', q_nope[:, q0:k_end], k_nope[:, :k_end])
             + jnp.einsum('bqhr,bkr->bhqk', q_rope[:, q0:k_end], k_rope[:, :k_end]))
        s = s.astype(jnp.float32) * scale
        causal = (q0 + jnp.arange(BLOCK_Q))[:, None] >= jnp.arange(k_end)[None, :]
        p = jax.nn.softmax(jnp.where(causal, s, -jnp.inf), axis=-1).astype(v.dtype)
        outs.append(jnp.einsum('bhqk,bkhd->bqhd', p, v[:, :k_end]))
    o = jnp.concatenate(outs, axis=1).reshape(B, S, MLA_WIDTH)
    return (o * jax.nn.silu(g)) @ w_out

def sb_mixer(h, w_in, w_out):
    B, S, _ = h.shape
    proj = h @ w_in
    q, k, v, g = jnp.split(proj, 4, axis=-1)
    q = q.reshape(B, S, SB_HEADS, SB_HEAD_DIM)
    k = k.reshape(B, S, SB_HEADS, SB_HEAD_DIM)
    v = v.reshape(B, S, SB_HEADS, SB_HEAD_DIM)
    scale = SB_HEAD_DIM ** -0.5
    outs = []
    for i in range(S // BLOCK_Q):
        q0, k_end = i * BLOCK_Q, (i + 1) * BLOCK_Q
        z = jnp.einsum('bqhd,bkhd->bhqk', q[:, q0:k_end], k[:, :k_end]).astype(jnp.float32) * scale
        strict = (q0 + jnp.arange(BLOCK_Q))[:, None] > jnp.arange(k_end)[None, :]
        log_beta = jax.nn.log_sigmoid(z)
        log_1m_beta = jnp.where(strict, jax.nn.log_sigmoid(-z), 0.0)
        after = lax.cumsum(log_1m_beta, axis=3, reverse=True) - log_1m_beta
        a = jnp.where(strict, jnp.exp(log_beta + after), 0.0).astype(v.dtype)
        outs.append(jnp.einsum('bhqk,bkhd->bqhd', a, v[:, :k_end]))
    o = jnp.concatenate(outs, axis=1).reshape(B, S, SB_WIDTH)
    return (o * jax.nn.silu(g)) @ w_out

def setup_inputs(seed: int = 0) -> dict:
    key = jax.random.key(seed)
    ks = jax.random.split(key, 20)

    def w(k, shape, fan_in):
        return jax.random.normal(k, shape, jnp.float32) * (fan_in ** -0.5)

    def gain(k, shape):
        return 1.0 + 0.01 * jax.random.normal(k, shape, jnp.float32)

    nA, nB, nC = N_GLA_LAYERS, N_MLA_LAYERS, N_SB_LAYERS
    return {
        "x": jax.random.normal(ks[0], (BATCH, SEQ, D_MODEL), jnp.float32),
        "norm_g": gain(ks[1], (DEPTH, D_MODEL)),
        "final_g": gain(ks[2], (D_MODEL,)),
        "gla_w_in": w(ks[3], (nA, D_MODEL, GLA_IN), D_MODEL),
        "gla_w_gate2": w(ks[4], (nA, GLA_GATE_RANK, GLA_KEY_DIM), GLA_GATE_RANK),
        "gla_b_gate": 0.1 * jax.random.normal(ks[5], (nA, GLA_KEY_DIM), jnp.float32),
        "gla_norm_g": gain(ks[6], (nA, GLA_DV)),
        "gla_w_out": w(ks[7], (nA, GLA_VAL_DIM, D_MODEL), GLA_VAL_DIM),
        "mla_w_in": w(ks[8], (nB, D_MODEL, MLA_IN), D_MODEL),
        "mla_q_norm_g": gain(ks[9], (nB, MLA_Q_RANK)),
        "mla_kv_norm_g": gain(ks[10], (nB, MLA_KV_RANK)),
        "mla_w_uq": w(ks[11], (nB, MLA_Q_RANK, MLA_HEADS * (MLA_NOPE + MLA_ROPE)), MLA_Q_RANK),
        "mla_w_ukv": w(ks[12], (nB, MLA_KV_RANK, MLA_HEADS * (MLA_NOPE + MLA_V)), MLA_KV_RANK),
        "mla_w_out": w(ks[13], (nB, MLA_WIDTH, D_MODEL), MLA_WIDTH),
        "sb_w_in": w(ks[14], (nC, D_MODEL, SB_IN), D_MODEL),
        "sb_w_out": w(ks[15], (nC, SB_WIDTH, D_MODEL), SB_WIDTH),
    }

def reference(x, norm_g, final_g, gla_w_in, gla_w_gate2, gla_b_gate, gla_norm_g, gla_w_out,
              mla_w_in, mla_q_norm_g, mla_kv_norm_g, mla_w_uq, mla_w_ukv, mla_w_out,
              sb_w_in, sb_w_out):
    cos, sin = rope_tables(x.shape[1], MLA_ROPE)
    for layer in range(DEPTH):
        kind, j = layer % N_MIXERS, layer // N_MIXERS
        h = rmsnorm(x, norm_g[layer])
        if kind == 0:
            y = gla_mixer(h, gla_w_in[j], gla_w_gate2[j], gla_b_gate[j], gla_norm_g[j], gla_w_out[j])
        elif kind == 1:
            y = mla_mixer(h, mla_w_in[j], mla_q_norm_g[j], mla_kv_norm_g[j], mla_w_uq[j],
                          mla_w_ukv[j], mla_w_out[j], cos, sin)
        else:
            y = sb_mixer(h, sb_w_in[j], sb_w_out[j])
        x = x + y
    return rmsnorm(x, final_g)


_drawn_inputs = setup_inputs


def setup_inputs(seed=0):
    import zlib

    import numpy as np

    out = dict(_drawn_inputs(seed))
    spreads = {}
    factors = {'norm_g': 2.99,
     'final_g': 5.568,
     'gla_norm_g': 6.571,
     'mla_q_norm_g': 8.0,
     'mla_kv_norm_g': 8.0}
    for name, (base, spread) in spreads.items():
        noise = np.random.default_rng([zlib.crc32(name.encode()), seed]).standard_normal(out[name].shape)
        drawn = base * np.exp(spread * noise) if base else spread * noise
        out[name] = __import__('jax').numpy.asarray(drawn.astype(out[name].dtype))
    for name, factor in factors.items():
        out[name] = (out[name] * factor).astype(out[name].dtype)
    return out
```

```python
from contextlib import ExitStack

import concourse.bass as bass
from concourse import mybir
from concourse.alu_op_type import AluOpType as ALU

ACT = mybir.ActivationFunctionType
F32 = mybir.dt.float32
F16 = mybir.dt.float16
AX_X = mybir.AxisListType.X

P = 128
D = 1024
KD = D // P
T = 1024
HALF = 512
TT = T // P
EPS = 1e-6
W_SCALE = 64.0
INV_W = 1.0 / W_SCALE
EXP_LN_TABLE = 6

GLA_HEADS, GLA_DK, GLA_DV, GLA_RANK = 4, 128, 256, 16
GLA_NORMALIZER = 16.0
GLA_SUB = 32
MLA_HEADS, MLA_NOPE, MLA_ROPE, MLA_V = 16, 128, 64, 128
MLA_QR, MLA_KVR = 256, 128
SB_HEADS, SB_DIM = 16, 64


def weave(main, filler, cost):
    total_weight = sum(item[1] for item in main if item[0] == "gap")
    total_cost = sum(cost(item) for item in filler)
    out, k, weight, spent = [], 0, 0, 0
    for item in main:
        if item[0] != "gap":
            out.append(item)
            continue
        weight += item[1]
        while k < len(filler) and (spent * total_weight < weight * total_cost):
            out.append(filler[k])
            spent += cost(filler[k])
            k += 1
    return out + filler[k:]


class Layer:

    NLOAD, NSPLIT = 2, 2
    PARTS = 4

    def __init__(self, nc, ctx, tag, net):
        self.nc, self.ctx, self.tag, self.net = nc, ctx, tag, net
        self.sems = []
        self.slabs = []
        self.units = []
        self.items = []
        self.last_unit_of = {}
        self.is_cut = set()
        sem, sb = self.sem, self.sb
        self.w_loaded = [sem(f"w_loaded{i}") for i in range(self.NLOAD)]
        self.w_hi_done, self.w_lo_done = sem("w_hi_done"), sem("w_lo_done")
        self.acc_ready = sem("acc_ready")
        self.acc_free = [sem(f"acc_free{b}") for b in range(8)]
        self.turn = []
        self.wf = [sb(f"wf{i}", [P, 1024], F32) for i in range(self.NLOAD)]
        self.w_hi = [sb(f"w_hi{i}", [P, 1024], F16) for i in range(self.NSPLIT)]
        self.w_lo = [sb(f"w_lo{i}", [P, 1024], F16) for i in range(self.NSPLIT)]

    def sem(self, name):
        s = self.ctx.enter_context(self.nc.semaphore(f"{self.tag}_{name}"))
        self.sems.append(s)
        return s

    def sb(self, name, shape, dt):
        return self.ctx.enter_context(self.nc.sbuf_tensor(f"{self.tag}_{name}", shape, dt))

    def slab(self, dram, cols, kinds, banks):
        s = len(self.slabs)
        self.slabs.append((dram, cols))
        out = [("w", s)]
        for kind, payload in kinds:
            n = len(self.units)
            b = banks[n % len(banks)]
            self.turn.append(1 + sum(u[3] == b for u in self.units))
            self.units.append((kind, payload, s, b))
            out.append(("u", n))
        self.last_unit_of[s] = len(self.units)
        return out

    def cut(self, items, names):
        out = []
        for it in items:
            if it[0] == "u" and self.units[it[1]][0] in names:
                self.is_cut.add(it[1])
                out += [("part", it[1], i) for i in range(self.PARTS - 1)]
            out.append(it)
        return out

    def open_early(self, items, units):
        out, rest, done = [], [], 0
        for it in items:
            early = it[0] != "u" and done < units
            (out if early else rest).append(it)
            done += it[0] == "part" and it[2] == self.PARTS - 2
        return out, rest

    def share(self, n, part, count):
        if n not in self.is_cut:
            return range(count)
        return range(count * part // self.PARTS, count * (part + 1) // self.PARTS)

    def finish_items(self, items):
        where = {it[1]: i for i, it in enumerate(items) if it[0] == "w"}
        moved = {}
        first = {}
        for i, it in enumerate(items):
            if it[0] in ("u", "part"):
                first.setdefault(self.units[it[1]][2], i)
        for s in where:
            moved.setdefault(first[s - 1] if s else 0, []).append(("w", s))
        out = []
        for i, it in enumerate(items):
            out += moved.get(i, [])
            if it[0] != "w":
                out.append(it)
        self.items = out

    def load_slab(self, sp, s):
        if s >= len(self.slabs):
            return
        dram, cols = self.slabs[s]
        if s >= self.NLOAD:
            sp.wait_ge(self.w_lo_done, s - self.NLOAD + 1)
            sp.wait_ge(self.w_hi_done, s - self.NLOAD + 1)
        sp.dma_start(self.wf[s % self.NLOAD][:, 0:cols], dram).then_inc(self.w_loaded[s % self.NLOAD], 16)

    def sync_w(self, sp, s):
        if s == 0:
            for k in range(self.NLOAD):
                self.load_slab(sp, k)
        elif s + self.NLOAD - 1 < len(self.slabs):
            self.load_slab(sp, s + self.NLOAD - 1)

    def act_w(self, act, s):
        cols = self.slabs[s][1]
        act.wait_ge(self.w_loaded[s % self.NLOAD], 16 * (s // self.NLOAD + 1))
        if s >= self.NSPLIT:
            act.wait_ge(self.acc_ready, self.last_unit_of[s - self.NSPLIT])
            act.wait_ge(self.w_lo_done, s - self.NSPLIT + 1)
        act.activation(self.w_hi[s % self.NSPLIT][:, 0:cols], self.wf[s % self.NLOAD][:, 0:cols],
                       ACT.Copy, scale=W_SCALE).then_inc(self.w_hi_done, 1)

    def dve_w(self, dve, s):
        cols = self.slabs[s][1]
        dve.wait_ge(self.w_hi_done, s + 1)
        dve.scalar_tensor_tensor(out=self.w_lo[s % self.NSPLIT][:, 0:cols],
                                 in0=self.wf[s % self.NLOAD][:, 0:cols], scalar=W_SCALE,
                                 in1=self.w_hi[s % self.NSPLIT][:, 0:cols],
                                 op0=ALU.mult, op1=ALU.subtract).then_inc(self.w_lo_done, 1)

    def wait_unit(self, eng, n):
        eng.wait_ge(self.acc_free[self.units[n][3]], self.turn[n])

    def bank(self, b):
        return self.net.psum[:, b, :]

    def pe_begin_unit(self, pe, n, part):
        kind, payload, s, b = self.units[n]
        if n in self.is_cut and part:
            return
        pe.wait_ge(self.w_lo_done, s + 1)
        if self.turn[n] > 1:
            pe.wait_ge(self.acc_free[b], self.turn[n] - 1)

    def pe_feature_major(self, pe, n, part, act_hi, act_lo, blocks, half, width=P, col=0, stride=P):
        _, _, s, b = self.units[n]
        wh, wl = self.w_hi[s % self.NSPLIT], self.w_lo[s % self.NSPLIT]
        out = self.bank(b)[0:width, :]
        tok = slice(half * HALF, half * HALF + HALF)
        last = len(blocks) - 1
        for i in self.share(n, part, len(blocks)):
            k = blocks[i]
            w = slice(i * stride + col, i * stride + col + width)
            pe.matmul(out, wh[:, w], act_hi[:, k, tok], start=(i == 0), stop=False)
            pe.matmul(out, wh[:, w], act_lo[:, k, tok], start=False, stop=False)
            mm = pe.matmul(out, wl[:, w], act_hi[:, k, tok], start=False, stop=(i == last))
            if i == last:
                mm.then_inc(self.acc_ready, 1)

    def pe_token_major(self, pe, n, part, act_hi, act_lo, blocks, half, col=0, stride=P):
        _, _, s, b = self.units[n]
        wh, wl = self.w_hi[s % self.NSPLIT], self.w_lo[s % self.NSPLIT]
        last = len(blocks) - 1
        for t in self.share(n, part, 4):
            tok = slice((4 * half + t) * P, (4 * half + t + 1) * P)
            out = self.bank(b)[:, t * P:(t + 1) * P]
            for i, k in enumerate(blocks):
                w = slice(i * stride + col, i * stride + col + P)
                pe.matmul(out, act_hi[:, k, tok], wh[:, w], start=(i == 0), stop=False)
                pe.matmul(out, act_hi[:, k, tok], wl[:, w], start=False, stop=False)
                mm = pe.matmul(out, act_lo[:, k, tok], wh[:, w], start=False, stop=(i == last))
            if t == 3:
                mm.then_inc(self.acc_ready, 1)


class Gate:

    def __init__(self, layer):
        L = self.layer = layer
        self.buf = [L.sb(f"gate_tmp{i}", [P, HALF], F32) for i in range(2)]
        self.clamped, self.sig = L.sem("gate_clamped"), L.sem("gate_sig")
        self.exp1, self.ln = L.sem("gate_exp"), L.sem("gate_ln")
        self.order = []

    def number(self, n):
        self.order.append(n)

    def dve_clamp(self, dve, n):
        L, i = self.layer, self.order.index(n)
        dve.wait_ge(L.acc_ready, n + 1)
        if i >= 2:
            m = self.order[i - 2]
            dve.wait_ge(L.acc_free[L.units[m][3]], L.turn[m])
        dve.tensor_scalar(self.buf[i % 2][:], L.bank(L.units[n][3]), INV_W, -40.0,
                          ALU.mult, ALU.max).then_inc(self.clamped, 1)

    def act(self, act, n):
        i = self.order.index(n)
        b = self.buf[i % 2][:]
        act.wait_ge(self.clamped, i + 1)
        act.activation(b, b, ACT.Exp, scale=-1.0).then_inc(self.exp1, 1)
        act.wait_ge(self.exp1, i + 1)
        act.activation(b, b, ACT.Ln, bias=1.0).then_inc(self.ln, 1)
        act.wait_ge(self.ln, i + 1)
        act.activation(b, b, ACT.Exp, scale=-1.0).then_inc(self.sig, 1)

    def dve_mult(self, dve, n, out):
        L, i = self.layer, self.order.index(n)
        dve.wait_ge(self.sig, i + 1)
        dve.scalar_tensor_tensor(out=out, in0=L.bank(L.units[n][3]), scalar=INV_W,
                                 in1=self.buf[i % 2][:], op0=ALU.mult,
                                 op1=ALU.mult).then_inc(L.acc_free[L.units[n][3]], 1)


class Rsqrt:

    def __init__(self, layer, name):
        self.m_ready, self.ln = layer.sem(f"{name}_m"), layer.sem(f"{name}_ln")
        self.guess, self.step = layer.sem(f"{name}_guess"), layer.sem(f"{name}_step")

    def dve_m(self, dve, m, s, scale):
        dve.tensor_scalar(m, s, scale, EPS, ALU.mult, ALU.add).then_inc(self.m_ready, 1)

    def act(self, act, i, m, r):
        act.wait_ge(self.m_ready, i + 1)
        act.activation(r, m, ACT.Ln).then_inc(self.ln, 1)
        act.wait_ge(self.ln, i + 1)
        act.activation(r, r, ACT.Exp, scale=-0.5).then_inc(self.guess, 1)

    def dve_newton(self, dve, i, m, r):
        dve.wait_ge(self.guess, i + 1)
        dve.tensor_tensor(m, m, r, ALU.mult).then_inc(self.step, 1)
        dve.wait_ge(self.step, 4 * i + 1)
        dve.tensor_tensor(m, m, r, ALU.mult).then_inc(self.step, 1)
        dve.wait_ge(self.step, 4 * i + 2)
        dve.tensor_scalar(m, m, -0.5, 1.5, ALU.mult, ALU.add).then_inc(self.step, 1)
        dve.wait_ge(self.step, 4 * i + 3)
        dve.tensor_tensor(r, r, m, ALU.mult).then_inc(self.step, 1)

    def wait_done(self, eng, i):
        eng.wait_ge(self.step, 4 * i + 4)


class Norm:

    def __init__(self, layer, gain, m, r, xr):
        L = self.layer = layer
        self.gain, self.m, self.r, self.xr = gain, m, r, xr
        self.total = L.sem("norm_total")
        self.rsqrt = Rsqrt(L, "norm")
        self.xr_ready = [L.sem("norm_xr_even"), L.sem("norm_xr_odd")]
        self.hi_ready, self.lo_ready = L.sem("norm_hi"), L.sem("norm_lo")

    def half(self, c):
        return slice(c * HALF, (c + 1) * HALF)

    def pe(self, pe):
        for c in range(2):
            pe.matmul(self.layer.bank(6 + c), self.layer.net.ones[:], self.layer.net.ssum[:, self.half(c)],
                      start=True, stop=True).then_inc(self.total, 1)

    def act(self, act):
        L = self.layer
        for c in range(2):
            self.rsqrt.act(act, c, self.m[:, self.half(c)], self.r[:, self.half(c)])
        for c in range(2):
            for k in range(KD):
                i = c * KD + k
                act.wait_ge(self.xr_ready[k % 2], i // 2 + 1)
                act.activation(L.net.h_hi[:, k, self.half(c)], self.xr[k % 4], ACT.Copy,
                               scale=self.gain[:, k:k + 1]).then_inc(self.hi_ready, 1)

    def make_xr(self, eng, c, k):
        i = c * KD + k
        self.rsqrt.wait_done(eng, c)
        if i >= 4:
            eng.wait_ge(self.lo_ready, i - 3)
        eng.tensor_tensor(self.xr[k % 4], self.layer.net.xT[:, k, self.half(c)],
                          self.r[:, self.half(c)], ALU.mult).then_inc(self.xr_ready[k % 2], 1)

    def pool(self, pool):
        for c in range(2):
            for k in range(0, KD, 2):
                self.make_xr(pool, c, k)

    def dve(self, dve):
        L = self.layer
        for c in range(2):
            dve.wait_ge(self.total, c + 1)
            self.rsqrt.dve_m(dve, self.m[:, self.half(c)], L.bank(6 + c), 1.0 / D)
        for c in range(2):
            self.rsqrt.dve_newton(dve, c, self.m[:, self.half(c)], self.r[:, self.half(c)])
            for k in range(KD):
                if k % 2:
                    self.make_xr(dve, c, k)
                if k >= 2:
                    self.lo(dve, c, k - 2)
            self.lo(dve, c, KD - 2)
            self.lo(dve, c, KD - 1)

    def lo(self, dve, c, k):
        dve.wait_ge(self.hi_ready, c * KD + k + 1)
        dve.scalar_tensor_tensor(out=self.layer.net.h_lo[:, k, self.half(c)], in0=self.xr[k % 4],
                                 scalar=self.gain[:, k:k + 1], in1=self.layer.net.h_hi[:, k, self.half(c)],
                                 op0=ALU.mult, op1=ALU.subtract).then_inc(self.lo_ready, 1)

    def wait_h(self, eng, c):
        eng.wait_ge(self.lo_ready, KD * (c + 1))


class Residual:

    def __init__(self, layer, sq):
        L = self.layer = layer
        self.sq = sq
        self.sq_ready, self.sum_ready = L.sem("sq_ready"), L.sem("sum_ready")

    def dve(self, dve, n):
        L = self.layer
        _, (k, c, *_), _, b = L.units[n]
        x = L.net.xT[:, k, c * HALF:(c + 1) * HALF]
        dve.wait_ge(L.acc_ready, n + 1)
        dve.scalar_tensor_tensor(out=x, in0=L.bank(b), scalar=INV_W, in1=x, op0=ALU.mult,
                                 op1=ALU.add).then_inc(L.acc_free[b], 1)

    def act(self, act, n):
        L = self.layer
        _, (k, c, final, *_), _, b = L.units[n]
        if not final:
            return
        act.wait_ge(L.acc_free[b], L.turn[n])
        i = 2 * k + c
        if k == 0:
            out = L.net.ssum[:, c * HALF:(c + 1) * HALF]
        else:
            out = self.sq[c][:]
            if k > 1:
                act.wait_ge(self.sum_ready, i - 3)
        act.activation(out, L.net.xT[:, k, c * HALF:(c + 1) * HALF], ACT.Square).then_inc(self.sq_ready, 1)

    def pool(self, pool, n):
        _, (k, c, final, *_), _, _ = self.layer.units[n]
        if not final or k == 0:
            return
        s = self.layer.net.ssum[:, c * HALF:(c + 1) * HALF]
        i = 2 * k + c
        pool.wait_ge(self.sq_ready, i + 1)
        if i >= 4:
            pool.wait_ge(self.sum_ready, i - 3)
        pool.tensor_tensor(s, s, self.sq[c][:], ALU.add).then_inc(self.sum_ready, 1)


class Split:

    def __init__(self, layer):
        self.layer = layer
        self.hi_ready = layer.sem("split_hi")
        self.order = []

    def number(self, n):
        self.order.append(n)

    def act(self, act, n, hi, scale, src=None):
        L = self.layer
        act.wait_ge(L.acc_ready, n + 1)
        act.activation(hi, L.bank(L.units[n][3]) if src is None else src, ACT.Copy,
                       scale=scale).then_inc(self.hi_ready, 1)

    def dve(self, dve, n, hi, lo, scale, src=None):
        L = self.layer
        b = L.units[n][3]
        dve.wait_ge(self.hi_ready, self.order.index(n) + 1)
        dve.scalar_tensor_tensor(out=lo, in0=L.bank(b) if src is None else src, scalar=scale, in1=hi,
                                 op0=ALU.mult, op1=ALU.subtract).then_inc(L.acc_free[b], 1)


def run_engines(nc, layer, program):
    with nc.Block() as block:
        @block.sync
        def _(sp):
            for item in layer.items:
                program.sync(sp, *item)

        @block.gpsimd
        def _(pool):
            for item in layer.items:
                program.pool(pool, *item)

        @block.scalar
        def _(act):
            for item in layer.items:
                program.act(act, *item)

        @block.vector
        def _(dve):
            for item in layer.items:
                program.dve(dve, *item)

        @block.tensor
        def _(pe):
            for item in layer.items:
                program.pe(pe, *item)


def clear_semaphores(nc, sems):
    numbers = sorted(s.num for s in sems)
    first = 0
    for i in range(1, len(numbers) + 1):
        if i == len(numbers) or numbers[i] != numbers[i - 1] + 1:
            nc.gpsimd.sem_clear(range(numbers[first], numbers[i - 1] + 1))
            first = i
    nc.all_engine_barrier()


class StickBreaking:
    PAIRS = SB_HEADS // 2
    SHIFT = 3
    STEPS = [(g, j) for g in range(2) for j in range(4 * g + 3, -1, -1)]

    def __init__(self, nc, net, tag, w_in, w_out, gain_row):
        self.nc, self.net = nc, net
        with ExitStack() as ctx:
            L = self.L = Layer(nc, ctx, tag, net)
            sb, sem = L.sb, L.sem
            self.y_hi, self.y_lo = sb("y_hi", [P, KD, T], F16), sb("y_lo", [P, KD, T], F16)
            self.q_hh = sb("q_hh", [P, 2, 2, T], F16)
            self.q_ll = sb("q_ll", [P, 2, 2, T], F16)
            self.k_hl = sb("k_hl", [P, 2, 2, T], F16)
            self.st_hi, self.st_lo = sb("st_hi", [P, T], F16), sb("st_lo", [P, T], F16)
            self.v_hi, self.v_lo = sb("v_hi", [P, 2, TT, P], F16), sb("v_lo", [P, 2, TT, P], F16)
            self.sg = sb("silu_g", [P, 2, T], F32)
            self.zc = [sb(f"zc{i}", [P, 2, HALF], F32) for i in range(3)]
            self.el, self.Lf = sb("el", [P, 2, HALF], F32), sb("Lf", [P, 2, HALF], F32)
            self.Lh = [sb(f"Lh{i}", [P, 2, HALF], F16) for i in range(2)]
            self.Ll = [sb(f"Ll{i}", [P, 2, HALF], F16) for i in range(2)]
            self.ah = [sb(f"ah{i}", [P, 2, HALF], F16) for i in range(2)]
            self.al = [sb(f"al{i}", [P, 2, HALF], F16) for i in range(2)]
            self.yt = sb("yt", [P, HALF], F32)
            self.later = sb("later_key", [P, P], F16)
            self.not_later = sb("not_later_key", [P, P], F16)
            self.mask = sb("strict_mask", [P, 2, P], F32)
            self.gain = sb("gain", [P, KD], F32)
            self.consts, self.gain_in = sem("consts"), sem("gain_in")
            self.gate = Gate(L)
            self.split = Split(L)
            self.resid = Residual(L, [self.zc[0][:, 0, :], self.zc[0][:, 1, :]])
            self.norm = Norm(L, self.gain, self.zc[0][:].rearrange("p a b -> p (a b)"),
                             self.zc[1][:].rearrange("p a b -> p (a b)"),
                             [self.zc[2][:, 0, :], self.zc[2][:, 1, :], self.el[:, 0, :], self.el[:, 1, :]])
            self.staged_sent = [sem("stacks_even"), sem("stacks_odd")]
            self.z_ready = sem("z_ready")
            self.zc_ready = sem("zc_ready")
            self.e_ready = sem("e_ready")
            self.l_ready = sem("l_ready")
            self.L_ready = sem("L_ready")
            self.Lm_ready = sem("Lm_ready")
            self.Lh_ready = sem("Lh_ready")
            self.Ll_ready = sem("Ll_ready")
            self.lb_ready = sem("lb_ready")
            self.lbm_ready = sem("lbm_ready")
            self.s_ready = sem("s_ready")
            self.arg_ready = sem("arg_ready")
            self.a_ready = sem("a_ready")
            self.ah_ready = sem("ah_ready")
            self.al_ready = sem("al_ready")
            self.pv_done = sem("pv_done")
            self.yt_ready = sem("yt_ready")
            self.yh_ready = sem("yh_ready")
            self.yl_ready = sem("yl_ready")
            self.gain_row = gain_row
            self.unit = {}
            self.build_items(w_in, w_out)
            run_engines(nc, L, self)
            clear_semaphores(nc, L.sems)

    def projections(self, p, w_in):
        L, out, later = self.L, [], []
        for name, sec in (("q", 0), ("k", 1), ("v", 2), ("g", 3)):
            for it in L.slab(w_in[sec * self.PAIRS + p], 1024, [(name, (p, c)) for c in range(2)], [5, 6, 7]):
                out.append(it)
                if it[0] != "u":
                    continue
                out += later
                later = []
                n = it[1]
                self.unit[name, p, L.units[n][1][1]] = n
                if name == "g":
                    self.gate.number(n)
                    later = [("g2", n)]
                else:
                    self.split.number(n)
            if name in "qk":
                out.append(("stack", name, p))
        return out + later

    def attention(self, p):
        steps = []
        for i in range(len(self.STEPS)):
            s = p * len(self.STEPS) + i
            more = s + 1 < self.PAIRS * len(self.STEPS)
            out = [("z", s + 1)] if more else []
            out.append(("t", s))
            if more:
                out.append(("l", s + 1))
            out += [("gap", 1), ("c", s), ("gap", 1), ("a", s)]
            if s >= 1:
                out.append(("pv", s - 1))
            steps.append(out)
        return steps

    def build_items(self, w_in, w_out):
        L = self.L
        filler = L.cut(self.projections(0, w_in), ("q", "k", "v", "g"))
        first_gate = next(i for i, it in enumerate(filler) if it[0] == "part" and L.units[it[1]][0] == "g") - 1
        items = [("start",)] + filler[:first_gate] + [("z", 0), ("l", 0)]
        filler = filler[first_gate:]
        main = []
        for p in range(self.PAIRS):
            for i, step in enumerate(self.attention(p)):
                if i == self.SHIFT:
                    items += weave(main, filler, lambda it: it[0] in ("u", "part"))
                    filler = L.cut(self.projections(p + 1, w_in), ("q", "k", "v", "g")) if p + 1 < self.PAIRS else []
                    main = []
                main += step
        last = []
        for k in range(KD):
            last += L.slab(w_out[k], 1024, [("x", (k, c, True)) for c in range(2)], [5, 6, 7])
        early, last = L.open_early(L.cut(last, ("x",)), 2)
        items += weave(main, early, lambda it: it[0] == "part")
        items += [("pv", self.PAIRS * len(self.STEPS) - 1)] + last
        L.finish_items(items)

    def where(self, s):
        p, i = divmod(s, len(self.STEPS))
        g, j = self.STEPS[i]
        off = max(0, j - 4 * g) * P
        return p, j == 4 * g + 3, j == 0, g, j, off

    def halves_before(self, s):
        p, i = divmod(s, len(self.STEPS))
        return 2 * p + (i >= 4)

    def pe(self, pe, kind, *a):
        L, net = self.L, self.net
        if kind == "start":
            pe.wait_ge(self.consts, 4)
            self.norm.pe(pe)
        elif kind in ("u", "part"):
            n, part = (*a, L.PARTS - 1)[:2]
            name, payload, _, _ = L.units[n]
            L.pe_begin_unit(pe, n, part)
            if name == "x":
                k, c, _ = payload
                pe.wait_ge(self.yl_ready, 2 * (L.share(n, part, KD)[-1] + 1))
                L.pe_feature_major(pe, n, part, self.y_hi, self.y_lo, range(KD), c)
                return
            p, c = payload
            if p == 0:
                self.norm.wait_h(pe, c)
            if name == "v":
                L.pe_token_major(pe, n, part, net.h_hi, net.h_lo, range(KD), c)
            else:
                L.pe_feature_major(pe, n, part, net.h_hi, net.h_lo, range(KD), c)
        elif kind == "z":
            s, = a
            p, _, _, g, j, off = self.where(s)
            pe.wait_ge(self.staged_sent[p % 2], 192 * (p // 2 + 1))
            if s >= 1:
                pe.wait_ge(self.L_ready, s)
            for h in range(2):
                out = L.bank(h)[:, off:HALF]
                k = self.k_hl[:, p % 2, h, j * P:(j + 1) * P]
                q = slice(g * HALF + off, (g + 1) * HALF)
                pe.matmul(out, k, self.q_hh[:, p % 2, h, q], start=True, stop=False)
                mm = pe.matmul(out, k, self.q_ll[:, p % 2, h, q], start=False, stop=True)
            mm.then_inc(self.z_ready, 1)
        elif kind == "t":
            s, = a
            _, first, _, _, _, off = self.where(s)
            pe.wait_ge(self.Ll_ready, s + 1)
            if s >= 1:
                pe.wait_ge(self.arg_ready, s)
            for h in range(2):
                out = L.bank(2 + h)[:, off:HALF]
                pe.matmul(out, self.later[:], self.Lh[s % 2][:, h, off:HALF], start=first, stop=False,
                          skip_group_check=True)
                mm = pe.matmul(out, self.later[:], self.Ll[s % 2][:, h, off:HALF], start=False, stop=True,
                               skip_group_check=True)
            mm.then_inc(self.s_ready, 1)
        elif kind == "c":
            s, = a
            _, _, last, _, _, off = self.where(s)
            if last:
                return
            pe.wait_ge(self.arg_ready, s + 1)
            for h in range(2):
                out = L.bank(2 + h)[:, off:HALF]
                for part in (self.Lh, self.Ll):
                    pe.matmul(out, self.not_later[:], part[s % 2][:, h, off:HALF], start=False, stop=True,
                              skip_group_check=True)
        elif kind == "pv":
            s, = a
            p, first, last, _, j, off = self.where(s)
            pe.wait_ge(self.al_ready, s + 1)
            if first:
                for c in range(2):
                    L.wait_unit(pe, self.unit["v", p, c])
                if self.halves_before(s) >= 1:
                    pe.wait_ge(self.yt_ready, self.halves_before(s))
            for h in range(2):
                out = L.bank(4)[h * SB_DIM:(h + 1) * SB_DIM, off:HALF]
                vh = self.v_hi[:, p % 2, j, h * SB_DIM:(h + 1) * SB_DIM]
                vl = self.v_lo[:, p % 2, j, h * SB_DIM:(h + 1) * SB_DIM]
                ah, al = self.ah[s % 2][:, h, off:HALF], self.al[s % 2][:, h, off:HALF]
                pe.matmul(out, vh, ah, start=first, stop=False, skip_group_check=True)
                pe.matmul(out, vl, ah, start=False, stop=False, skip_group_check=True)
                mm = pe.matmul(out, vh, al, start=False, stop=last, skip_group_check=True)
            mm.then_inc(self.pv_done, 1)

    def dve(self, dve, kind, *a):
        L, net = self.L, self.net
        if kind == "start":
            dve.wait_ge(self.gain_in, 16)
            self.norm.dve(dve)
        elif kind == "w":
            L.dve_w(dve, *a)
        elif kind == "u":
            n, = a
            name, payload, _, b = L.units[n]
            if name == "x":
                self.resid.dve(dve, n)
                return
            p, c = payload
            half = slice(c * HALF, (c + 1) * HALF)
            if name in ("q", "k"):
                self.split.dve(dve, n, self.st_hi[:, half], self.st_lo[:, half], self.scale_of(name))
            elif name == "v":
                self.split.dve(dve, n, self.v_hi[:, p % 2, 4 * c:4 * c + 4, :].rearrange("p t d -> p (t d)"),
                               self.v_lo[:, p % 2, 4 * c:4 * c + 4, :].rearrange("p t d -> p (t d)"), INV_W)
            else:
                self.gate.dve_clamp(dve, n)
        elif kind == "g2":
            n, = a
            p, c = L.units[n][1]
            if p >= 2:
                dve.wait_ge(self.yt_ready, 2 * (p - 1))
            self.gate.dve_mult(dve, n, self.sg[:, p % 2, c * HALF:(c + 1) * HALF])
        elif kind == "z":
            s, = a
            off = self.where(s)[-1]
            z = L.net.psum[:, 0:2, off:HALF]
            dve.wait_ge(self.z_ready, s + 1)
            if s >= 3:
                dve.wait_ge(self.al_ready, s - 2)
            dve.tensor_scalar(self.zc[s % 3][:, :, off:HALF], z, 40.0, None, ALU.min).then_inc(self.zc_ready, 1)
        elif kind == "l":
            s, = a
            p, first, last, g, j, off = self.where(s)
            z = L.net.psum[:, 0:2, off:HALF]
            lf = self.Lf[:, :, off:HALF]
            dve.wait_ge(self.l_ready, s + 1)
            if s >= 1:
                dve.wait_ge(self.Ll_ready, s)
            dve.tensor_tensor(lf, z, self.el[:, :, off:HALF], ALU.max).then_inc(self.L_ready, 1)
            dve.wait_ge(self.L_ready, s + 1)
            if j >= 4 * g:
                d = self.Lf[:, :, off:off + P]
                dve.tensor_tensor(d, d, self.mask[:], ALU.mult).then_inc(self.Lm_ready, 1)
            dve.wait_ge(self.Lh_ready, s + 1)
            dve.tensor_tensor(self.Ll[s % 2][:, :, off:HALF], lf, self.Lh[s % 2][:, :, off:HALF],
                              ALU.subtract).then_inc(self.Ll_ready, 1)
        elif kind == "t":
            s, = a
            off = self.where(s)[-1]
            lb = self.zc[s % 3][:, :, off:HALF]
            dve.wait_ge(self.s_ready, s + 1)
            self.wait_lb(dve, s)
            dve.tensor_tensor(lb, lb, net.psum[:, 2:4, off:HALF], ALU.subtract).then_inc(self.arg_ready, 1)
        elif kind == "pv":
            s, = a
            if self.where(s)[2]:
                self.dve_y(dve, s)

    def diag_count(self, s):
        return sum(j >= 4 * g for g, j in self.STEPS) * (s // len(self.STEPS)) + \
            sum(j >= 4 * g for g, j in self.STEPS[:s % len(self.STEPS) + 1])

    def wait_lb(self, eng, s):
        _, _, _, g, j, _ = self.where(s)
        if j >= 4 * g:
            eng.wait_ge(self.lbm_ready, self.diag_count(s))
        eng.wait_ge(self.lb_ready, s + 1)

    def scale_of(self, name):
        return INV_W * SB_DIM ** -0.5 if name == "q" else INV_W

    def dve_y(self, dve, s):
        p, _, _, g, _, _ = self.where(s)
        n = 2 * p + g
        dve.wait_ge(self.pv_done, s + 1)
        self.L.wait_unit(dve, self.unit["g", p, g])
        if n >= 1:
            dve.wait_ge(self.yl_ready, n)
        dve.tensor_tensor(self.yt[:], self.L.bank(4), self.sg[:, p % 2, g * HALF:(g + 1) * HALF],
                          ALU.mult).then_inc(self.yt_ready, 1)

    def act(self, act, kind, *a):
        L, net = self.L, self.net
        if kind == "start":
            act.wait_ge(self.gain_in, 16)
            self.norm.act(act)
        elif kind == "w":
            L.act_w(act, *a)
        elif kind == "u":
            n, = a
            name, payload, _, b = L.units[n]
            if name == "x":
                if n == L.last_unit_of[4 * self.PAIRS - 1]:
                    act.wait_ge(self.al_ready, self.PAIRS * len(self.STEPS))
                self.resid.act(act, n)
                return
            p, c = payload
            half = slice(c * HALF, (c + 1) * HALF)
            if name in ("q", "k"):
                if name == "k":
                    act.wait_ge(self.staged_sent[p % 2], 192 * (p // 2) + 128)
                elif p >= 1:
                    act.wait_ge(self.staged_sent[(p - 1) % 2], 192 * ((p - 1) // 2 + 1))
                self.split.act(act, n, self.st_hi[:, half], self.scale_of(name))
            elif name == "v":
                if p >= 2:
                    act.wait_ge(self.pv_done, len(self.STEPS) * (p - 1))
                self.split.act(act, n, self.v_hi[:, p % 2, 4 * c:4 * c + 4, :].rearrange("p t d -> p (t d)"), INV_W)
            else:
                self.gate.act(act, n)
        elif kind == "z":
            s, = a
            off = self.where(s)[-1]
            el = self.el[:, :, off:HALF]
            act.wait_ge(self.zc_ready, s + 1)
            if s >= 1:
                act.wait_ge(self.L_ready, s)
                act.wait_ge(self.lb_ready, s)
            act.activation(el, self.zc[s % 3][:, :, off:HALF], ACT.Exp).then_inc(self.e_ready, 1)
            act.wait_ge(self.e_ready, s + 1)
            act.activation(el, el, ACT.Ln, bias=1.0).then_inc(self.l_ready, 1)
        elif kind == "t":
            s, = a
            off = self.where(s)[-1]
            arg = self.zc[s % 3][:, :, off:HALF]
            act.wait_ge(self.arg_ready, s + 1)
            act.activation(arg, arg, ACT.Exp).then_inc(self.a_ready, 1)
        elif kind == "l":
            s, = a
            p, _, _, g, j, off = self.where(s)
            act.wait_ge(self.L_ready, s + 1)
            if j >= 4 * g:
                act.wait_ge(self.Lm_ready, self.diag_count(s))
            if s >= 2:
                act.wait_ge(self.s_ready, s)
            act.activation(self.Lh[s % 2][:, :, off:HALF], self.Lf[:, :, off:HALF],
                           ACT.Copy).then_inc(self.Lh_ready, 1)
        elif kind == "a":
            s, = a
            off = self.where(s)[-1]
            act.wait_ge(self.a_ready, s + 1)
            if s >= 2:
                act.wait_ge(self.pv_done, s - 1)
            act.activation(self.ah[s % 2][:, :, off:HALF], self.zc[s % 3][:, :, off:HALF],
                           ACT.Copy).then_inc(self.ah_ready, 1)
        elif kind == "pv":
            s, = a
            p, _, last, g, _, _ = self.where(s)
            if last:
                act.wait_ge(self.yt_ready, 2 * p + g + 1)
                act.activation(self.y_hi[:, p, g * HALF:(g + 1) * HALF], self.yt[:],
                               ACT.Copy).then_inc(self.yh_ready, 1)

    def pool(self, pool, kind, *a):
        L = self.L
        if kind == "start":
            for tile in (self.later, self.not_later):
                pool.memset(tile[:], 1.0).then_inc(self.consts, 1)
            pool.memset(self.mask[:], 1.0).then_inc(self.consts, 1)
            pool.wait_ge(self.consts, 3)
            pool.affine_select(out=self.later[:], in_=self.later[:], compare_op=ALU.is_gt, fill=0.0, base=0,
                               pattern=[[-1, P]], channel_multiplier=1)
            pool.affine_select(out=self.not_later[:], in_=self.not_later[:], compare_op=ALU.is_ge, fill=0.0,
                               base=0, pattern=[[1, P]], channel_multiplier=-1)
            pool.affine_select(out=self.mask[:], in_=self.mask[:], compare_op=ALU.is_gt, fill=0.0, base=0,
                               pattern=[[0, 2], [1, P]], channel_multiplier=-1).then_inc(self.consts, 1)
            self.norm.pool(pool)
        elif kind == "u":
            if L.units[a[0]][0] == "x":
                self.resid.pool(pool, a[0])
        elif kind == "l":
            s, = a
            _, _, _, g, j, off = self.where(s)
            lb = self.zc[s % 3]
            pool.wait_ge(self.l_ready, s + 1)
            pool.tensor_tensor(lb[:, :, off:HALF], lb[:, :, off:HALF], self.el[:, :, off:HALF],
                               ALU.subtract).then_inc(self.lb_ready, 1)
            if j >= 4 * g:
                pool.wait_ge(self.lb_ready, s + 1)
                pool.affine_select(out=lb[:, :, off:off + P], in_=lb[:, :, off:off + P], compare_op=ALU.is_gt,
                                   fill=-1e30, base=0, pattern=[[0, 2], [1, P]],
                                   channel_multiplier=-1).then_inc(self.lbm_ready, 1)
        elif kind == "a":
            s, = a
            off = self.where(s)[-1]
            pool.wait_ge(self.ah_ready, s + 1)
            pool.tensor_tensor(self.al[s % 2][:, :, off:HALF], self.zc[s % 3][:, :, off:HALF],
                               self.ah[s % 2][:, :, off:HALF], ALU.subtract).then_inc(self.al_ready, 1)
        elif kind == "pv":
            s, = a
            p, _, last, g, _, _ = self.where(s)
            if last:
                pool.wait_ge(self.yh_ready, 2 * p + g + 1)
                y = slice(g * HALF, (g + 1) * HALF)
                pool.tensor_tensor(self.y_lo[:, p, y], self.yt[:], self.y_hi[:, p, y],
                                   ALU.subtract).then_inc(self.yl_ready, 1)

    def sync(self, sp, kind, *a):
        L = self.L
        if kind == "start":
            sp.dma_start(self.gain[:], self.gain_row).then_inc(self.gain_in, 16)
        elif kind == "w":
            L.sync_w(sp, *a)
        elif kind == "stack":
            name, p = a
            for c in range(2):
                L.wait_unit(sp, self.unit[name, p, c])
            if p >= 2:
                sp.wait_ge(self.z_ready, len(self.STEPS) * (p - 1))
            hi, lo = self.st_hi, self.st_lo
            for h in range(2):
                rows = slice(h * SB_DIM, (h + 1) * SB_DIM)
                if name == "q":
                    pairs = [(self.q_hh, 0, hi), (self.q_hh, 1, hi), (self.q_ll, 0, lo), (self.q_ll, 1, lo)]
                else:
                    pairs = [(self.k_hl, 0, hi), (self.k_hl, 1, lo)]
                for dst, part, src in pairs:
                    sp.dma_start(dst[part * SB_DIM:(part + 1) * SB_DIM, p % 2, h, :],
                                 src[rows, :]).then_inc(self.staged_sent[p % 2], 16)


class LatentAttention:
    GROUP = 4
    SCALE = (MLA_NOPE + MLA_ROPE) ** -0.5
    MASK = -60000.0
    MASK_GAIN = 32768.0

    def __init__(self, nc, net, tag, w, gain_row, q_gain, kv_gain, rope):
        self.nc, self.net, self.w = nc, net, w
        self.rows = (gain_row, q_gain, kv_gain, rope)
        with ExitStack() as ctx:
            L = self.L = Layer(nc, ctx, tag, net)
            sb, sem = L.sb, L.sem
            self.y_hi, self.y_lo = sb("y_hi", [P, 2 * self.GROUP, T], F16), sb("y_lo", [P, 2 * self.GROUP, T], F16)
            self.qn_hi, self.qn_lo = sb("qn_hi", [P, 2, T], F16), sb("qn_lo", [P, 2, T], F16)
            self.kn_hi, self.kn_lo = sb("kn_hi", [P, 2, T], F16), sb("kn_lo", [P, 2, T], F16)
            self.v_hi, self.v_lo = sb("v_hi", [P, 2, TT, P], F16), sb("v_lo", [P, 2, TT, P], F16)
            self.sg = sb("silu_g", [P, T], F32)
            self.qr = sb("qr_stack", [P, 4, T], F16)
            self.prob = [sb(f"prob{i}", [P, T], F32) for i in range(2)]
            self.pt_hi = [sb(f"pt_hi{i}", [P, T], F16) for i in range(2)]
            self.pt_lo = [sb(f"pt_lo{i}", [P, T], F16) for i in range(2)]
            self.cq_hi, self.cq_lo = sb("cq_hi", [P, 2, T], F16), sb("cq_lo", [P, 2, T], F16)
            self.ckv_hi, self.ckv_lo = sb("ckv_hi", [P, 1, T], F16), sb("ckv_lo", [P, 1, T], F16)
            self.kr_hh, self.kr_ll = sb("kr_hh", [P, T], F16), sb("kr_ll", [P, T], F16)
            self.cos, self.sin = sb("cos", [P, T], F32), sb("sin", [P, T], F32)
            self.rt = [sb(f"rt{i}", [P, HALF], F32) for i in range(2)]
            self.st_hi, self.st_lo = sb("st_hi", [P, HALF], F16), sb("st_lo", [P, HALF], F16)
            self.yt = sb("yt", [P, HALF], F32)
            self.ident = sb("ident", [P, P], F32)
            self.mask_w, self.mask_k = sb("mask_w", [P, P], F16), sb("mask_k", [P, P], F16)
            self.diag = [sb(f"diag{i}", [P, P], F32) for i in range(2)]
            self.gain, self.cgain = sb("gain", [P, KD], F32), sb("cgain", [P, 3], F32)
            self.top, self.neg_top = sb("top", [P, 4], F32), sb("neg_top", [P, 4], F32)
            self.total, self.inv_total = sb("total", [P, 4], F32), sb("inv_total", [P, 4], F32)
            yh = self.y_hi[:].rearrange("p a b -> p (a b)").bitcast(F32)
            yl = self.y_lo[:].rearrange("p a b -> p (a b)").bitcast(F32)
            self.cf, self.csq = yh[:, 0:3 * T], yl[:, 0:3 * T]
            self.cm = [self.prob[0], self.prob[1]]
            self.cr = [yh[:, 3 * T:4 * T], yl[:, 3 * T:4 * T]]
            self.kt = [t[:].bitcast(F32) for t in (*self.pt_hi, *self.pt_lo)]

            self.gate, self.split = Gate(L), Split(L)
            self.resid = Residual(L, [self.rt[0], self.rt[1]])
            self.norm = Norm(L, self.gain, self.prob[0][:], self.prob[1][:], [self.rt[0][:], self.rt[1][:], self.sg[:, 0:HALF], self.sg[:, HALF:T]])
            self.crs = Rsqrt(L, "latent")
            self.consts, self.gain_in, self.rope_in = sem("consts"), sem("gain_in"), sem("rope_in")
            self.csq_ready, self.ctot, self.cr_ready = sem("csq_ready"), sem("ctot"), sem("cr_ready")
            self.chi, self.clo = sem("chi"), sem("clo")
            self.ra_ready, self.rsum, self.rhi, self.rlo = sem("ra_ready"), sem("rsum"), sem("rhi"), sem("rlo")
            self.stacked = [sem("stacked_even"), sem("stacked_odd")]
            self.s_ready, self.top_ready, self.neg_ready = sem("s_ready"), sem("top_ready"), sem("neg_ready")
            self.p_ready, self.inv_ready, self.diag_ready = sem("p_ready"), sem("inv_ready"), sem("diag_ready")
            self.t_ready, self.pth_ready, self.ptl_ready = sem("t_ready"), sem("pth_ready"), sem("ptl_ready")
            self.pv_done, self.yt_ready = sem("pv_done"), sem("yt_ready")
            self.yh_ready, self.yl_ready = sem("yh_ready"), sem("yl_ready")
            self.unit, self.ropes, self.group_end = {}, [], {}
            self.build_items()
            run_engines(nc, L, self)
            clear_semaphores(nc, L.sems)

    ACC = [5, 6, 7]
    def pe_cost(self, item):
        if item[0] not in ("u", "part"):
            return 0
        name = self.L.units[item[1]][0]
        return {"x": 12, "g": 24, "qn": 24, "kn": 12, "v": 12, "qA": 24, "qB": 24}[name]

    def add_slab(self, dram, cols, units):
        L, out, later = self.L, [], []
        for it in L.slab(dram, cols, units, self.ACC):
            out.append(it)
            if it[0] != "u":
                continue
            out += later
            later = []
            n = it[1]
            name, payload, _, _ = L.units[n]
            self.unit[(name, *payload)] = n
            if name == "g":
                self.gate.number(n)
                later = [("g2", n)]
            elif name in ("qn", "kn", "v"):
                self.split.number(n)
            elif name in ("qB", "kB"):
                self.ropes.append((name[0], *payload))
                out.append(("rope", len(self.ropes) - 1))
        return out + later

    def gate_items(self, h):
        return self.add_slab(self.w["gate"][h], 1024, [("g", (h, c)) for c in range(2)])

    def head_items(self, h):
        out = []
        if h % 2 == 0:
            out += self.add_slab(self.w["q_rope"][h // 2], 512,
                                 [(n, (h // 2, c)) for c in range(2) for n in ("qA", "qB")])
        return out + self.add_slab(self.w["up"][h], 512, [(n, (h, c)) for n in ("qn", "kn", "v") for c in range(2)])

    def out_items(self, group, part):
        final = group == MLA_HEADS // self.GROUP - 1
        items = self.L.slab(self.w["out"][group * 4 + part], 1024,
                            [("x", (2 * part + k, c, final, group)) for k in range(2) for c in range(2)], self.ACC)
        self.group_end[group] = len(self.L.units)
        return items

    def build_items(self):
        L = self.L
        items = [("start",)]
        for b in range(3):
            items += self.add_slab(self.w["latent"][b], 1024, [("c", (b, c)) for c in range(2)])
        items += self.add_slab(self.w["latent"][3], 1024, [("kA", (0, c)) for c in range(2)])
        items += self.add_slab(self.w["latent"][4], 1024, [("kB", (0, c)) for c in range(2)])
        items.append(("latent",))
        items += self.gate_items(0) + self.head_items(0)
        last = MLA_HEADS * TT - 1
        items += [("s", 0), ("m", 0)]
        main, filler = [], []
        for t in range(last + 1):
            h, i = divmod(t, TT)
            if i == 0:
                if h:
                    filler += self.gate_items(h)
                if h >= self.GROUP:
                    filler += self.out_items(h // self.GROUP - 1, h % self.GROUP)
                values = []
                if h + 1 < MLA_HEADS:
                    new = self.head_items(h + 1)
                    filler += new[:-2]
                    values = new[-2:]
            if i == TT - 1:
                items += weave(main, L.cut(filler, ("x", "g")), self.pe_cost)
                main, filler = [], list(values)
            main += [("s", t + 1)] if t < last else []
            main += [("d", t)]
            main += [("m", t + 1)] if t < last else []
            main += [("t", t), ("e", t), ("gap", 1)]
            main += [("pv", t - 1)] if t else []
        items += [it for it in main if it[0] != "gap"]
        tail = []
        for part in range(4):
            tail += self.out_items(MLA_HEADS // self.GROUP - 1, part)
        early, tail = L.open_early(L.cut(tail, ("x",)), 3)
        items += early + [("pv", last)] + tail
        L.finish_items(self.place_gates(items))

    def place_gates(self, items):
        out, waiting, units, done = [], [], 0, -1

        def release(ready):
            for g in [g for g in waiting if ready(g)]:
                waiting.remove(g)
                out.append(("g2", g[0]))

        for item in items:
            if item[0] == "g2":
                continue
            if item[0] == "pv":
                release(lambda g: g[3] <= item[1])
                done = item[1]
            out.append(item)
            if item[0] == "u":
                units += 1
                if self.L.units[item[1]][0] == "g":
                    h, c = self.L.units[item[1]][1]
                    waiting.append((item[1], units, h * TT - 1, h * TT + 4 * c + 3))
            release(lambda g: units > g[1] and done >= g[2])
        return out

    def pair(self, t):
        b = 2 * (t % 2)
        return self.net.psum[:, b:b + 2, :].rearrange("p a b -> p (a b)")

    def pe(self, pe, kind, *a):
        L, net = self.L, self.net
        if kind == "start":
            pe.wait_ge(self.consts, 5)
            self.norm.pe(pe)
        elif kind in ("u", "part"):
            n, part = (*a, L.PARTS - 1)[:2]
            name, payload, _, _ = L.units[n]
            L.pe_begin_unit(pe, n, part)
            c = payload[1]
            if name == "x":
                group = payload[3]
                heads = self.GROUP * group + L.share(n, part, self.GROUP)[-1] + 1
                pe.wait_ge(self.yl_ready, 2 * heads)
                k0 = self.GROUP * (group % 2)
                L.pe_feature_major(pe, n, part, self.y_hi[:, k0:k0 + 4, :], self.y_lo[:, k0:k0 + 4, :], range(self.GROUP),
                                   c, col=(payload[0] % 2) * P, stride=2 * P)
            elif name in ("c", "kA", "kB", "g"):
                self.norm.wait_h(pe, c)
                L.pe_feature_major(pe, n, part, net.h_hi, net.h_lo, range(KD), c)
            else:
                pe.wait_ge(self.clo, 6)
                if name in ("qA", "qB", "qn"):
                    L.pe_feature_major(pe, n, part, self.cq_hi, self.cq_lo, range(2), c, col=2 * P * (name == "qB"))
                elif name == "kn":
                    L.pe_feature_major(pe, n, part, self.ckv_hi, self.ckv_lo, range(1), c, col=2 * P)
                else:
                    L.pe_token_major(pe, n, part, self.ckv_hi, self.ckv_lo, range(1), c, col=3 * P)
        elif kind == "latent":
            for part in range(2):
                blocks = ((0, 1), (2,))[part]
                for c in range(2):
                    pe.wait_ge(self.csq_ready, 2 * blocks[-1] + c + 1)
                    for b in blocks:
                        sq = self.csq[:, b * T + c * HALF:b * T + (c + 1) * HALF]
                        mm = pe.matmul(L.bank(2 * part + c), net.ones[:], sq, start=(b == blocks[0]),
                                       stop=(b == blocks[-1]))
                    mm.then_inc(self.ctot, 1)
        elif kind == "s":
            t, = a
            h, i = divmod(t, TT)
            if i == 0:
                for name in ("qn", "kn"):
                    for c in range(2):
                        L.wait_unit(pe, self.unit[name, h, c])
                pe.wait_ge(self.stacked[(h // 2) % 2], 128 * (h // 4 + 1))
                pe.wait_ge(self.rlo, 2)
            if t >= 2:
                pe.wait_ge(self.ptl_ready, t - 1)
            elif t == 0:
                pe.wait_ge(self.crs.step, 16)
            q = slice(i * P, (i + 1) * P)
            w = (i + 1) * P
            for k0 in range(0, w, HALF):
                k = slice(k0, min(w, k0 + HALF))
                out = self.pair(t)[:, k]
                diagonal = w - k0 <= HALF
                pe.matmul(out, self.qn_hi[:, h % 2, q], self.kn_hi[:, h % 2, k], start=True, stop=False)
                pe.matmul(out, self.qn_lo[:, h % 2, q], self.kn_hi[:, h % 2, k], start=False, stop=False)
                pe.matmul(out, self.qn_hi[:, h % 2, q], self.kn_lo[:, h % 2, k], start=False, stop=False)
                if diagonal:
                    pe.matmul(self.pair(t)[:, w - P:w], self.mask_w[:], self.mask_k[:], start=False, stop=False)
                pe.matmul(out, self.qr[:, h % 4, q], self.kr_hh[:, k], start=False, stop=False)
                mm = pe.matmul(out, self.qr[:, h % 4, q], self.kr_ll[:, k], start=False, stop=True)
            mm.then_inc(self.s_ready, 1)
        elif kind == "t":
            t, = a
            pe.wait_ge(self.diag_ready, t + 1)
            for j in range(t % TT + 1):
                mm = pe.matmul(self.pair(t)[:, j * P:(j + 1) * P], self.prob[t % 2][:, j * P:(j + 1) * P],
                               self.diag[t % 2][:], start=True, stop=True)
            mm.then_inc(self.t_ready, 1)
        elif kind == "pv":
            t, = a
            h, i = divmod(t, TT)
            pe.wait_ge(self.ptl_ready, t + 1)
            if i == 0:
                for c in range(2):
                    L.wait_unit(pe, self.unit["v", h, c])
            if i % 4 == 0 and t:
                pe.wait_ge(self.yt_ready, t // 4)
            out = L.bank(4)[:, (i % 4) * P:(i % 4 + 1) * P]
            for j in range(i + 1):
                key = slice(j * P, (j + 1) * P)
                vh, vl = self.v_hi[:, h % 2, j, :], self.v_lo[:, h % 2, j, :]
                pe.matmul(out, vh, self.pt_hi[t % 2][:, key], start=(j == 0), stop=False)
                pe.matmul(out, vl, self.pt_hi[t % 2][:, key], start=False, stop=False)
                mm = pe.matmul(out, vh, self.pt_lo[t % 2][:, key], start=False, stop=(j == i))
            mm.then_inc(self.pv_done, 1)

    def dests(self, name, h, c):
        half = slice(c * HALF, (c + 1) * HALF)
        if name == "v":
            return [v[:, h % 2, 4 * c:4 * c + 4, :].rearrange("p t d -> p (t d)") for v in (self.v_hi, self.v_lo)]
        hi, lo = (self.qn_hi, self.qn_lo) if name == "qn" else (self.kn_hi, self.kn_lo)
        return [hi[:, h % 2, half], lo[:, h % 2, half]]

    def rope_buffers(self, r):
        which, _, c = self.ropes[r]
        if which == "k":
            half = slice(c * HALF, (c + 1) * HALF)
            return self.kt[c], self.kt[2 + c], self.kr_hh[:, half], self.kr_ll[:, half]
        return self.rt[0][:], self.rt[1][:], self.st_hi[:], self.st_lo[:]

    def dve(self, dve, kind, *a):
        L, net = self.L, self.net
        if kind == "start":
            dve.wait_ge(self.gain_in, 48)
            self.norm.dve(dve)
        elif kind == "w":
            L.dve_w(dve, *a)
        elif kind == "latent":
            for part in range(2):
                for c in range(2):
                    dve.wait_ge(self.ctot, 2 * part + c + 1)
                    self.crs.dve_m(dve, self.cm[part][:, c * HALF:(c + 1) * HALF], L.bank(2 * part + c),
                                   1.0 / (MLA_QR, MLA_KVR)[part])
            for part in range(2):
                for c in range(2):
                    half = slice(c * HALF, (c + 1) * HALF)
                    self.crs.dve_newton(dve, 2 * part + c, self.cm[part][:, half], self.cr[part][:, half])
            for i in range(6):
                b, c = divmod(i, 2)
                dve.wait_ge(self.chi, i + 1)
                hi, lo, src = self.latent_parts(b, c)
                dve.scalar_tensor_tensor(out=lo, in0=src, scalar=self.cgain[:, b:b + 1], in1=hi,
                                         op0=ALU.mult, op1=ALU.subtract).then_inc(self.clo, 1)
        elif kind == "u":
            n, = a
            name, payload, _, b = L.units[n]
            c = payload[1]
            half = slice(c * HALF, (c + 1) * HALF)
            if name == "x":
                self.resid.dve(dve, n)
            elif name == "c":
                dve.wait_ge(L.acc_ready, n + 1)
                dve.tensor_scalar(self.cf[:, payload[0] * T + c * HALF:payload[0] * T + (c + 1) * HALF], L.bank(b),
                                  INV_W, None, ALU.mult).then_inc(L.acc_free[b], 1)
            elif name[1:] in ("A", "B"):
                r = 2 * payload[0] + c + (2 if name[0] == "q" else 0)
                table = self.cos if name[1] == "A" else self.sin
                out = self.rope_buffers_of(name[0], c)[name[1] == "B"]
                dve.wait_ge(self.rope_in, 32)
                dve.wait_ge(L.acc_ready, n + 1)
                if name[0] == "q" and r >= 3:
                    dve.wait_ge(self.rlo, r)
                dve.scalar_tensor_tensor(out=out, in0=L.bank(b), scalar=INV_W, in1=table[:, half],
                                         op0=ALU.mult, op1=ALU.mult).then_inc(L.acc_free[b], 1)
            elif name == "g":
                self.gate.dve_clamp(dve, n)
            else:
                hi, lo = self.dests(name, payload[0], c)
                self.split.dve(dve, n, hi, lo, INV_W)
        elif kind == "g2":
            n, = a
            h, c = L.units[n][1]
            if h:
                dve.wait_ge(self.yt_ready, 2 * h)
            self.gate.dve_mult(dve, n, self.sg[:, c * HALF:(c + 1) * HALF])
        elif kind == "rope":
            r, = a
            s, _, hi, lo = self.rope_buffers(r)
            dve.wait_ge(self.rhi, r + 1)
            dve.tensor_tensor(lo, s, hi, ALU.subtract).then_inc(self.rlo, 1)
        elif kind == "m":
            t, = a
            w = (t % TT + 1) * P
            k = slice(t % 4, t % 4 + 1)
            dve.wait_ge(self.s_ready, t + 1)
            if t >= 4:
                dve.wait_ge(self.neg_ready, t - 3)
            dve.reduce_max(self.top[:, k], self.pair(t)[:, 0:w], AX_X).then_inc(self.top_ready, 1)
            dve.wait_ge(self.top_ready, t + 1)
            if t >= 4:
                dve.wait_ge(self.p_ready, t - 3)
            dve.tensor_scalar(self.neg_top[:, k], self.top[:, k], -self.SCALE, None,
                              ALU.mult).then_inc(self.neg_ready, 1)
        elif kind == "d":
            t, = a
            k = slice(t % 4, t % 4 + 1)
            dve.wait_ge(self.p_ready, t + 1)
            if t >= 4:
                dve.wait_ge(self.diag_ready, t - 3)
            dve.reciprocal(self.inv_total[:, k], self.total[:, k]).then_inc(self.inv_ready, 1)
            dve.wait_ge(self.inv_ready, t + 1)
            if t >= 2:
                dve.wait_ge(self.t_ready, t - 1)
            dve.tensor_scalar(self.diag[t % 2][:], self.ident[:], self.inv_total[:, k], None,
                              ALU.mult).then_inc(self.diag_ready, 1)
        elif kind == "e":
            t, = a
            w = (t % TT + 1) * P
            dve.wait_ge(self.pth_ready, t + 1)
            dve.tensor_tensor(self.pt_lo[t % 2][:, 0:w], self.pair(t)[:, 0:w], self.pt_hi[t % 2][:, 0:w],
                              ALU.subtract).then_inc(self.ptl_ready, 1)
        elif kind == "pv":
            t, = a
            if t % 4 == 3:
                h, c = divmod(t // 4, 2)
                dve.wait_ge(self.pv_done, t + 1)
                L.wait_unit(dve, self.unit["g", h, c])
                if t >= 4:
                    dve.wait_ge(self.yl_ready, t // 4)
                dve.tensor_tensor(self.yt[:], L.bank(4), self.sg[:, c * HALF:(c + 1) * HALF],
                                  ALU.mult).then_inc(self.yt_ready, 1)

    def rope_buffers_of(self, which, c):
        return (self.kt[c], self.kt[2 + c]) if which == "k" else (self.rt[0][:], self.rt[1][:])

    def latent_parts(self, b, c):
        half = slice(c * HALF, (c + 1) * HALF)
        src = self.cf[:, b * T + c * HALF:b * T + (c + 1) * HALF]
        if b < 2:
            return self.cq_hi[:, b, half], self.cq_lo[:, b, half], src
        return self.ckv_hi[:, 0, half], self.ckv_lo[:, 0, half], src

    def act(self, act, kind, *a):
        L, net = self.L, self.net
        if kind == "start":
            act.wait_ge(self.gain_in, 48)
            self.norm.act(act)
        elif kind == "w":
            L.act_w(act, *a)
        elif kind == "latent":
            for part in range(2):
                for c in range(2):
                    half = slice(c * HALF, (c + 1) * HALF)
                    self.crs.act(act, 2 * part + c, self.cm[part][:, half], self.cr[part][:, half])
            for i in range(6):
                b, c = divmod(i, 2)
                act.wait_ge(self.cr_ready, i + 1)
                hi, _, src = self.latent_parts(b, c)
                act.activation(hi, src, ACT.Copy, scale=self.cgain[:, b:b + 1]).then_inc(self.chi, 1)
        elif kind == "u":
            n, = a
            name, payload, _, b = L.units[n]
            c = payload[1]
            if name == "x":
                self.act_x(act, n)
            elif name == "c":
                L.wait_unit(act, n)
                at = slice(payload[0] * T + c * HALF, payload[0] * T + (c + 1) * HALF)
                act.activation(self.csq[:, at], self.cf[:, at], ACT.Square).then_inc(self.csq_ready, 1)
            elif name == "g":
                self.gate.act(act, n)
            elif name in ("qn", "kn", "v"):
                h = payload[0]
                if h >= 2:
                    if name == "v":
                        act.wait_ge(self.pv_done, TT * (h - 1))
                    else:
                        act.wait_ge(self.s_ready, TT * (h - 1))
                self.split.act(act, n, self.dests(name, h, c)[0], INV_W)
        elif kind == "rope":
            r, = a
            s, _, hi, lo = self.rope_buffers(r)
            which, p, c = self.ropes[r]
            act.wait_ge(self.rsum, r + 1)
            if r >= 3:
                before = self.ropes[r - 1][1]
                act.wait_ge(self.stacked[before % 2], 128 * (before // 2) + 64 * (self.ropes[r - 1][2] + 1))
            act.activation(hi, s, ACT.Copy).then_inc(self.rhi, 1)
        elif kind == "m":
            t, = a
            w = (t % TT + 1) * P
            k = slice(t % 4, t % 4 + 1)
            act.wait_ge(self.neg_ready, t + 1)
            if t >= 2:
                act.wait_ge(self.t_ready, t - 1)
            if t >= 4:
                act.wait_ge(self.inv_ready, t - 3)
            act.activation(self.prob[t % 2][:, 0:w], self.pair(t)[:, 0:w], ACT.Exp, bias=self.neg_top[:, k],
                           scale=self.SCALE, accum_out=self.total[:, k]).then_inc(self.p_ready, 1)
        elif kind == "e":
            t, = a
            w = (t % TT + 1) * P
            act.wait_ge(self.t_ready, t + 1)
            if t >= 2:
                act.wait_ge(self.pv_done, t - 1)
            act.activation(self.pt_hi[t % 2][:, 0:w], self.pair(t)[:, 0:w], ACT.Copy).then_inc(self.pth_ready, 1)
        elif kind == "pv":
            t, = a
            if t % 4 == 3:
                h, c = divmod(t // 4, 2)
                act.wait_ge(self.yt_ready, t // 4 + 1)
                if h >= 2 * self.GROUP:
                    act.wait_ge(L.acc_ready, self.group_end[h // self.GROUP - 2])
                act.activation(self.y_hi[:, h % (2 * self.GROUP), c * HALF:(c + 1) * HALF], self.yt[:],
                               ACT.Copy).then_inc(self.yh_ready, 1)

    def act_x(self, act, n):
        k, c, final, group = self.L.units[n][1]
        if final and (k, c) in ((0, 0), (1, 0)):
            act.wait_ge(self.rlo, len(self.ropes))
        self.resid.act(act, n)

    def pool(self, pool, kind, *a):
        L, net = self.L, self.net
        if kind == "start":
            pool.memset(self.ident[:], 1.0).then_inc(self.consts, 1)
            pool.memset(self.mask_w[:], self.MASK_GAIN).then_inc(self.consts, 1)
            pool.memset(self.mask_k[:], self.MASK).then_inc(self.consts, 1)
            pool.wait_ge(self.consts, 3)
            for tile in (self.ident, self.mask_w):
                pool.affine_select(out=tile[:], in_=tile[:], compare_op=ALU.is_equal, fill=0.0, base=0,
                                   pattern=[[-1, P]], channel_multiplier=1).then_inc(self.consts, 1)
            pool.affine_select(out=self.mask_k[:], in_=self.mask_k[:], compare_op=ALU.is_gt, fill=0.0, base=0,
                               pattern=[[1, P]], channel_multiplier=-1).then_inc(self.consts, 1)
            self.norm.pool(pool)
        elif kind == "latent":
            for i in range(6):
                b, c = divmod(i, 2)
                part = int(b == 2)
                self.crs.wait_done(pool, 2 * part + c)
                src = self.latent_parts(b, c)[2]
                pool.tensor_tensor(src, src, self.cr[part][:, c * HALF:(c + 1) * HALF],
                                   ALU.mult).then_inc(self.cr_ready, 1)
        elif kind == "rope":
            r, = a
            which, p, c = self.ropes[r]
            s, b, _, _ = self.rope_buffers(r)
            L.wait_unit(pool, self.unit[which + "A", p, c])
            L.wait_unit(pool, self.unit[which + "B", p, c])
            pool.tensor_tensor(s, s, b, ALU.add).then_inc(self.rsum, 1)
        elif kind == "u":
            if L.units[a[0]][0] == "x":
                self.resid.pool(pool, a[0])
        elif kind == "pv":
            t, = a
            if t % 4 == 3:
                h, c = divmod(t // 4, 2)
                at = slice(c * HALF, (c + 1) * HALF)
                slot = h % (2 * self.GROUP)
                pool.wait_ge(self.yh_ready, t // 4 + 1)
                pool.tensor_tensor(self.y_lo[:, slot, at], self.yt[:], self.y_hi[:, slot, at],
                                   ALU.subtract).then_inc(self.yl_ready, 1)

    def sync(self, sp, kind, *a):
        L = self.L
        if kind == "start":
            gain_row, q_gain, kv_gain, rope = self.rows
            sp.dma_start(self.gain[:], gain_row).then_inc(self.gain_in, 16)
            sp.dma_start(self.cgain[:, 0:2], q_gain).then_inc(self.gain_in, 16)
            sp.dma_start(self.cgain[:, 2:3], kv_gain).then_inc(self.gain_in, 16)
            sp.dma_start(self.cos[:], rope[0]).then_inc(self.rope_in, 16)
            sp.dma_start(self.sin[:], rope[1]).then_inc(self.rope_in, 16)
        elif kind == "w":
            L.sync_w(sp, *a)
        elif kind == "rope":
            r, = a
            which, p, c = self.ropes[r]
            if which == "k":
                return
            sp.wait_ge(self.rlo, r + 1)
            if p >= 2:
                sp.wait_ge(self.s_ready, 2 * TT * (p - 1))
            half = slice(c * HALF, (c + 1) * HALF)
            for j in range(2):
                rows = slice(j * MLA_ROPE, (j + 1) * MLA_ROPE)
                for part, src in enumerate((self.st_hi, self.st_lo)):
                    sp.dma_start(self.qr[part * MLA_ROPE:(part + 1) * MLA_ROPE, (2 * p + j) % 4, half],
                                 src[rows, :]).then_inc(self.stacked[p % 2], 16)


class GatedLinear:
    NC = T // P
    NSUB = P // GLA_SUB
    ACC = [0, 1]

    def __init__(self, nc, net, tag, w, gain_row, head_gain):
        self.nc, self.net, self.w = nc, net, w
        self.rows = (gain_row, head_gain)
        with ExitStack() as ctx:
            L = self.L = Layer(nc, ctx, tag, net)
            sb, sem = L.sb, L.sem
            self.y_hi, self.y_lo = sb("y_hi", [P, KD, T], F16), sb("y_lo", [P, KD, T], F16)
            self.q, self.k = sb("q", [P, T], F32), sb("k", [P, T], F32)
            self.v = sb("v", [P, 2, TT, GLA_DV], F32)
            self.sg = sb("silu_g", [P, 2, T], F32)
            self.sp = sb("softplus", [P, TT, GLA_HEADS * GLA_DK], F32)
            self.a_low = self.sg[0:32, 0, :]
            self.wg2 = self.sg[0:GLA_RANK + 1, 1, 0:GLA_HEADS * GLA_DK]
            self.b = sb("decay_sum", [P, T], F32)
            self.e = [sb(f"e{i}", [P, T], F32) for i in range(2)]
            self.qe, self.kt = sb("qe", [P, T], F32), sb("kt", [P, T], F32)
            self.kd = sb("kd_token_major", [P, self.NC, GLA_DK], F32)
            self.at = sb("attn_T", [P, self.NC, P], F32)
            self.state = sb("state", [P, self.NC, GLA_DV], F32)
            self.blast = sb("exp_b_last", [P, self.NC], F32)
            self.tri, self.ident = sb("tri", [P, P], F32), sb("ident", [P, P], F32)
            self.mask = sb("mask", [P, P], F32)
            self.gain, self.hgain = sb("gain", [P, KD], F32), sb("hgain", [P, 2], F32)
            self.qt = self.e[1]

            self.gate = Gate(L)
            self.resid = Residual(L, [self.e[0][:, 0:HALF], self.e[0][:, HALF:T]])
            self.norm = Norm(L, self.gain, self.e[0][:], self.e[1][:], [t[:, c * HALF:(c + 1) * HALF] for t in (self.qe, self.kt) for c in range(2)])
            self.ors = Rsqrt(L, "head_norm")
            self.consts, self.gain_in = sem("consts"), sem("gain_in")
            self.lg_ready, self.lg_c, self.lg_e, self.lg_l, self.sp_ready = (
                sem("lg_ready"), sem("lg_c"), sem("lg_e"), sem("lg_l"), sem("sp_ready"))
            self.b_psum, self.b_ready, self.argk, self.ek, self.kt_ready = (
                sem("b_psum"), sem("b_ready"), sem("argk"), sem("ek"), sem("kt_ready"))
            self.eq, self.blast_ready, self.qe_ready = sem("eq"), sem("blast_ready"), sem("qe_ready")
            self.argd, self.ed, self.kd_feat, self.kd_psum, self.kd_ready = (
                sem("argd"), sem("ed"), sem("kd_feat"), sem("kd_psum"), sem("kd_ready"))
            self.argq, self.eqt, self.qt_ready, self.a_psum, self.a_ready = (
                sem("argq"), sem("eqt"), sem("qt_ready"), sem("a_psum"), sem("a_ready"))
            self.kv_psum, self.state_ready, self.o_psum = sem("kv_psum"), sem("state_ready"), sem("o_psum")
            self.osq, self.osum, self.ototal = sem("osq"), sem("osum"), sem("ototal")
            self.on_ready, self.yt_ready, self.yh_ready, self.yl_ready = (
                sem("on_ready"), sem("yt_ready"), sem("yh_ready"), sem("yl_ready"))
            self.unit = {}
            self.build_items()
            run_engines(nc, L, self)
            clear_semaphores(nc, L.sems)

    def add_slab(self, dram, cols, units):
        L, out, later = self.L, [], []
        for it in L.slab(dram, cols, units, self.ACC):
            out.append(it)
            if it[0] == "u":
                n = it[1]
                name, payload, _, _ = L.units[n]
                self.unit[(name, *payload)] = n
                out += later
                later = []
                if name == "g":
                    self.gate.number(n)
                    later = [("g2", n)]
        return out + later

    def project(self, name, h, d=None):
        if name in ("q", "k"):
            return self.add_slab(self.w[name][h], 1024, [(name, (h, c)) for c in range(2)])
        return self.add_slab(self.w[name][2 * h + d], 1024, [(name, (h, c, d)) for c in range(2)])

    def build_items(self):
        L = self.L
        items = [("start",)] + self.add_slab(self.w["a_low"], KD * GLA_RANK, [("a_low", (0, c)) for c in range(2)])
        names, cost = ("q", "k", "v", "g"), lambda it: it[0] in ("u", "part")
        ahead = self.project("q", 0) + self.project("k", 0) + self.project("v", 0, 0) + self.project("v", 0, 1)
        main = []
        for i in range(TT):
            main += [("gap", 1), ("lg", i)]
        items += weave(main + [("gap", 1)], L.cut(ahead, names), cost)
        for h in range(GLA_HEADS):
            main = [("b", h), ("gap", 2), ("ek", h), ("eq", h), ("gap", 3), ("ed", h), ("aq", h, 0), ("gap", 4)]
            for j in range(self.NSUB):
                main += [("a", h, j)]
                if j == 0:
                    main += [("edT", h)]
                if j + 1 < self.NSUB:
                    main += [("aq", h, j + 1)]
                main += [("gap", 3)]
            filler = self.project("g", h, 0) + self.project("g", h, 1)
            if h + 1 < GLA_HEADS:
                filler += self.project("v", h + 1, 0)
            items += weave(main, L.cut(filler, names), cost)
            main = [("kv", h), ("gap", 4), ("o", h), ("sq", h), ("gap", 5), ("on", h), ("gap", 4), ("y", h, 0),
                    ("gap", 2), ("y", h, 1), ("gap", 4)]
            if h + 1 < GLA_HEADS:
                filler = L.cut(self.project("v", h + 1, 1) + self.project("q", h + 1) + self.project("k", h + 1), names)
                items += weave(main, filler, cost)
        last = []
        for k in range(KD):
            last += L.slab(self.w["out"][k], 1024, [("x", (k, c, True)) for c in range(2)], self.ACC)
        early, last = L.open_early(L.cut(last, ("x",)), 2)
        items += weave(main, early, cost) + last
        L.finish_items(items)

    def banks(self, b, n=2):
        return self.net.psum[:, b:b + n, :].rearrange("p a b -> p (a b)")

    def kv_out(self, c):
        return self.net.psum[:, (2, 3, 6, 7)[c // 2], (c % 2) * GLA_DV:(c % 2 + 1) * GLA_DV]

    def pe(self, pe, kind, *a):
        L, net = self.L, self.net
        if kind == "start":
            pe.wait_ge(self.consts, 7)
            self.norm.pe(pe)
        elif kind in ("u", "part"):
            n, part = (*a, L.PARTS - 1)[:2]
            name, payload, _, _ = L.units[n]
            L.pe_begin_unit(pe, n, part)
            if name == "x":
                pe.wait_ge(self.yl_ready, L.share(n, part, KD)[-1] + 1)
                L.pe_feature_major(pe, n, part, self.y_hi, self.y_lo, range(KD), payload[1])
                return
            c = payload[1]
            self.norm.wait_h(pe, c)
            if name == "a_low":
                L.pe_feature_major(pe, n, part, net.h_hi, net.h_lo, range(KD), c, width=GLA_RANK, stride=GLA_RANK)
            elif name == "v":
                L.pe_token_major(pe, n, part, net.h_hi, net.h_lo, range(KD), c)
            else:
                L.pe_feature_major(pe, n, part, net.h_hi, net.h_lo, range(KD), c)
        elif kind == "lg":
            i, = a
            pe.wait_ge(self.gain_in, 64)
            L.wait_unit(pe, self.unit["a_low", 0, 0])
            L.wait_unit(pe, self.unit["a_low", 0, 1])
            if i >= 2:
                pe.wait_ge(self.sp_ready, i - 1)
            pe.matmul(L.bank(2 + i % 2), self.a_low[0:GLA_RANK + 1, i * P:(i + 1) * P], self.wg2,
                      start=True, stop=True).then_inc(self.lg_ready, 1)
        elif kind == "b":
            h, = a
            pe.wait_ge(self.sp_ready, TT)
            if h:
                pe.wait_ge(self.ors.step, 8 * h)
            for c in range(self.NC):
                mm = pe.matmul(self.banks(2)[:, c * P:(c + 1) * P], self.sp[:, c, h * GLA_DK:(h + 1) * GLA_DK],
                               self.tri[:], start=True, stop=True)
            mm.then_inc(self.b_psum, 1)
        elif kind == "edT":
            h, = a
            pe.wait_ge(self.kd_feat, h + 1)
            if h:
                pe.wait_ge(self.on_ready, 2 * h)
            for c in range(self.NC):
                mm = pe.transpose(self.banks(6)[:, c * P:(c + 1) * P], self.e[0][:, c * P:(c + 1) * P], self.ident[:])
            mm.then_inc(self.kd_psum, 1)
        elif kind == "a":
            h, j = a
            i = h * self.NSUB + j
            pe.wait_ge(self.qt_ready, i + 1)
            pe.wait_ge(self.kt_ready, h + 1)
            if h and j == 0:
                pe.wait_ge(self.on_ready, 2 * h)
            lo = j * GLA_SUB
            for c in range(self.NC):
                keys = slice(c * P + lo, c * P + lo + GLA_SUB)
                out = self.banks(4)[lo:lo + GLA_SUB, c * P + lo:(c + 1) * P]
                mm = pe.matmul(out, self.kt[:, keys], self.qt[:, c * (P - lo):(c + 1) * (P - lo)], start=True, stop=True)
            mm.then_inc(self.a_psum, 1)
        elif kind == "kv":
            h, = a
            pe.wait_ge(self.kd_ready, h + 1)
            pe.wait_ge(self.b_ready, h + 1)
            for c in range(2):
                for d in range(2):
                    L.wait_unit(pe, self.unit["v", h, c, d])
            for c in range(self.NC - 1):
                pe.matmul(self.kv_out(c), self.kd[:, c, :], self.v[:, h % 2, c, :], start=True,
                          stop=True).then_inc(self.kv_psum, 1)
        elif kind == "o":
            h, = a
            pe.wait_ge(self.a_ready, self.NSUB * (h + 1))
            pe.wait_ge(self.state_ready, 7 * (h + 1))
            pe.wait_ge(self.qe_ready, h + 1)
            for d in range(2):
                cols = slice(d * P, (d + 1) * P)
                for c in range(self.NC):
                    out = self.banks(4 + 2 * d)[:, c * P:(c + 1) * P]
                    mm = pe.matmul(out, self.v[:, h % 2, c, cols], self.at[:, c, :], start=True, stop=(c == 0))
                    if c:
                        mm = pe.matmul(out, self.state[:, c, cols], self.qe[:, c * P:(c + 1) * P],
                                       start=False, stop=True)
                mm.then_inc(self.o_psum, 1)
        elif kind == "on":
            h, = a
            pe.wait_ge(self.osum, h + 1)
            for c in range(2):
                pe.matmul(L.bank(2 + c), net.ones[:], self.e[0][:, c * HALF:(c + 1) * HALF], start=True,
                          stop=True).then_inc(self.ototal, 1)

    def ref(self, j):
        b = self.b[:].rearrange("p (c t) -> p c t", t=P)
        m = j * GLA_SUB + GLA_SUB // 2
        return b[:, :, m:m + 1]

    def dve(self, dve, kind, *a):
        L, net = self.L, self.net
        if kind == "start":
            dve.wait_ge(self.gain_in, 64)
            self.norm.dve(dve)
        elif kind == "w":
            L.dve_w(dve, *a)
        elif kind == "u":
            n, = a
            name, payload, _, b = L.units[n]
            c = payload[1]
            if name == "x":
                self.resid.dve(dve, n)
                return
            if name == "g":
                self.gate.dve_clamp(dve, n)
                return
            if name == "v":
                return
            dve.wait_ge(L.acc_ready, n + 1)
            h, half = payload[0], slice(c * HALF, (c + 1) * HALF)
            if name == "a_low":
                dve.wait_ge(self.consts, 7)
                out, src, scale = self.a_low[0:GLA_RANK, half], L.bank(b)[0:GLA_RANK, :], INV_W
            else:
                if h:
                    dve.wait_ge(self.kd_feat, h)
                    dve.wait_ge(self.kt_ready, h)
                    dve.wait_ge(self.qe_ready, h)
                    dve.wait_ge(self.qt_ready, self.NSUB * h)
                out, src = (self.q if name == "q" else self.k)[:, half], L.bank(b)
                scale = INV_W * GLA_DK ** -0.5 if name == "q" else INV_W
            dve.tensor_scalar(out, src, scale, None, ALU.mult).then_inc(L.acc_free[b], 1)
        elif kind == "g2":
            n, = a
            h, c, d = L.units[n][1]
            if h:
                dve.wait_ge(self.yt_ready, 2 * h)
            else:
                dve.wait_ge(self.sp_ready, TT)
            self.gate.dve_mult(dve, n, self.sg[:, d, c * HALF:(c + 1) * HALF])
        elif kind == "lg":
            i, = a
            dve.wait_ge(self.lg_ready, i + 1)
            if i >= 2:
                dve.wait_ge(self.sp_ready, i - 1)
            buf = self.e[0][:, (i % 2) * HALF:(i % 2 + 1) * HALF]
            dve.tensor_scalar(buf, L.bank(2 + i % 2), -40.0, None, ALU.max).then_inc(self.lg_c, 1)
            dve.wait_ge(self.lg_l, i + 1)
            dve.scalar_tensor_tensor(out=self.sp[:, i, :], in0=L.bank(2 + i % 2), scalar=-1.0, in1=buf,
                                     op0=ALU.mult, op1=ALU.max).then_inc(self.sp_ready, 1)
        elif kind == "b":
            h, = a
            dve.wait_ge(self.b_psum, h + 1)
            if h:
                dve.wait_ge(self.yl_ready, 2 * h)
                dve.wait_ge(self.eq, h)
                dve.wait_ge(self.argd, h)
                dve.wait_ge(self.argq, self.NSUB * h)
                dve.wait_ge(self.blast_ready, h)
            dve.tensor_copy(self.b[:], self.banks(2)).then_inc(self.b_ready, 1)
        elif kind == "ek":
            h, = a
            dve.wait_ge(self.b_ready, h + 1)
            if h:
                dve.wait_ge(self.ototal, 2 * h)
            b4 = self.b[:].rearrange("p (c j t) -> p (c j) t", j=self.NSUB, t=GLA_SUB)
            e4 = self.e[0][:].rearrange("p (c j t) -> p (c j) t", j=self.NSUB, t=GLA_SUB)
            m = GLA_SUB // 2
            dve.tensor_tensor(e4, b4[:, :, m:m + 1].broadcast_to([P, self.NC * self.NSUB, GLA_SUB]), b4,
                              ALU.subtract).then_inc(self.argk, 1)
            dve.wait_ge(self.ek, h + 1)
            if h:
                dve.wait_ge(self.a_psum, self.NSUB * h)
            dve.tensor_tensor(self.kt[:], self.k[:], self.e[0][:], ALU.mult).then_inc(self.kt_ready, 1)
        elif kind == "ed":
            h, = a
            b3 = self.b[:].rearrange("p (c t) -> p c t", t=P)
            dve.wait_ge(self.kt_ready, h + 1)
            dve.tensor_tensor(self.e[0][:].rearrange("p (c t) -> p c t", t=P),
                              b3[:, :, P - 1:P].broadcast_to([P, self.NC, P]), b3,
                              ALU.subtract).then_inc(self.argd, 1)
            dve.wait_ge(self.ed, h + 1)
            dve.tensor_tensor(self.e[0][:], self.k[:], self.e[0][:], ALU.mult).then_inc(self.kd_feat, 1)
        elif kind == "aq":
            h, j = a
            i = h * self.NSUB + j
            n = P - j * GLA_SUB
            view = self.qt[:, 0:self.NC * n].rearrange("p (c t) -> p c t", t=n)
            b3 = self.b[:].rearrange("p (c t) -> p c t", t=P)[:, :, P - n:P]
            q3 = self.q[:].rearrange("p (c t) -> p c t", t=P)[:, :, P - n:P]
            if i:
                dve.wait_ge(self.a_psum, i)
            if j == 0:
                dve.wait_ge(self.qe_ready, h + 1)
                if h:
                    dve.wait_ge(self.osum, h)
            dve.tensor_tensor(view, b3, self.ref(j).broadcast_to([P, self.NC, n]), ALU.subtract).then_inc(self.argq, 1)
            dve.wait_ge(self.eqt, i + 1)
            dve.tensor_tensor(view, view, q3, ALU.mult).then_inc(self.qt_ready, 1)
        elif kind == "a":
            h, j = a
            i = h * self.NSUB + j
            n = P - j * GLA_SUB
            dve.wait_ge(self.a_psum, i + 1)
            rows = slice(j * GLA_SUB, (j + 1) * GLA_SUB)
            if h:
                dve.wait_ge(self.o_psum, 2 * h)
            ps = self.banks(4)[rows, :].rearrange("p (c t) -> p c t", t=P)[:, :, P - n:P]
            dve.tensor_tensor(self.at[rows, :, P - n:P], ps,
                              self.mask[rows, P - n:P].unsqueeze(1).broadcast_to([GLA_SUB, self.NC, n]),
                              ALU.mult).then_inc(self.a_ready, 1)
        elif kind == "kv":
            h, = a
            dve.wait_ge(self.blast_ready, h + 1)
            if h:
                dve.wait_ge(self.o_psum, 2 * h)
            for c in range(self.NC - 1):
                dve.wait_ge(self.kv_psum, 7 * h + min(7, 2 * (c // 2) + 2))
                if c == 0:
                    dve.tensor_copy(self.state[:, 1, :], self.kv_out(0)).then_inc(self.state_ready, 1)
                    continue
                dve.wait_ge(self.state_ready, 7 * h + c)
                dve.scalar_tensor_tensor(out=self.state[:, c + 1, :], in0=self.state[:, c, :],
                                         scalar=self.blast[:, c:c + 1], in1=self.kv_out(c), op0=ALU.mult,
                                         op1=ALU.add).then_inc(self.state_ready, 1)
        elif kind == "sq":
            h, = a
            dve.wait_ge(self.osq, 2 * h + 2)
            dve.tensor_tensor(self.e[0][:], self.e[0][:], self.e[1][:], ALU.add).then_inc(self.osum, 1)
        elif kind == "on":
            h, = a
            for c in range(2):
                half = slice(c * HALF, (c + 1) * HALF)
                dve.wait_ge(self.ototal, 2 * h + c + 1)
                self.ors.dve_m(dve, self.e[1][:, half], L.bank(2 + c), 1.0 / GLA_DV)
            for c in range(2):
                half = slice(c * HALF, (c + 1) * HALF)
                self.ors.dve_newton(dve, 2 * h + c, self.e[1][:, half], self.kt[:, half])
            self.ors.wait_done(dve, 2 * h + 1)
            for d in range(2):
                if d == 0:
                    dve.wait_ge(self.o_psum, 2 * h + 2)
                out = (self.qe, self.b)[d]
                dve.tensor_tensor(out[:], self.banks(4 + 2 * d), self.kt[:], ALU.mult).then_inc(self.on_ready, 1)
        elif kind == "y":
            h, d = a
            n = 2 * h + d
            src = (self.qe, self.b)[d]
            dve.wait_ge(self.on_ready, n + 1)
            for c in range(2):
                L.wait_unit(dve, self.unit["g", h, c, d])
            dve.scalar_tensor_tensor(out=src[:], in0=src[:], scalar=self.hgain[:, d:d + 1], in1=self.sg[:, d, :],
                                     op0=ALU.mult, op1=ALU.mult).then_inc(self.yt_ready, 1)
            dve.wait_ge(self.yh_ready, n + 1)
            dve.tensor_tensor(self.y_lo[:, n, :], src[:], self.y_hi[:, n, :], ALU.subtract).then_inc(self.yl_ready, 1)

    def act(self, act, kind, *a):
        L, net = self.L, self.net
        if kind == "start":
            act.wait_ge(self.gain_in, 64)
            self.norm.act(act)
        elif kind == "w":
            L.act_w(act, *a)
        elif kind == "u":
            n, = a
            name, payload, _, b = L.units[n]
            if name == "g":
                self.gate.act(act, n)
            elif name == "v":
                h, c, d = payload
                act.wait_ge(L.acc_ready, n + 1)
                if h >= 2:
                    act.wait_ge(self.o_psum, 2 * (h - 1))
                act.activation(self.v[:, h % 2, 4 * c:4 * c + 4, d * P:(d + 1) * P],
                               L.bank(b).rearrange("p (t d) -> p t d", d=P), ACT.Copy,
                               scale=INV_W).then_inc(L.acc_free[b], 1)
            elif name == "x":
                self.resid.act(act, a[0])
        elif kind == "lg":
            i, = a
            buf = self.e[0][:, (i % 2) * HALF:(i % 2 + 1) * HALF]
            act.wait_ge(self.lg_c, i + 1)
            act.activation(buf, buf, ACT.Exp, scale=-1.0).then_inc(self.lg_e, 1)
            act.wait_ge(self.lg_e, i + 1)
            act.activation(buf, buf, ACT.Ln, bias=1.0).then_inc(self.lg_l, 1)
        elif kind == "ek":
            h, = a
            act.wait_ge(self.argk, h + 1)
            act.activation(self.e[0][:], self.e[0][:], ACT.Exp).then_inc(self.ek, 1)
        elif kind == "eq":
            h, = a
            act.wait_ge(self.b_ready, h + 1)
            if h:
                act.wait_ge(self.on_ready, 2 * h)
            last = self.b[:].rearrange("p (c t) -> p c t", t=P)[:, :, P - 1:P]
            act.activation(self.blast[:].unsqueeze(2), last, ACT.Exp).then_inc(self.blast_ready, 1)
            act.activation(self.e[1][:], self.b[:], ACT.Exp).then_inc(self.eq, 1)
        elif kind == "ed":
            h, = a
            act.wait_ge(self.argd, h + 1)
            act.activation(self.e[0][:], self.e[0][:], ACT.Exp).then_inc(self.ed, 1)
        elif kind == "edT":
            h, = a
            act.wait_ge(self.kd_psum, h + 1)
            if h:
                act.wait_ge(self.kv_psum, 7 * h)
            act.activation(self.kd[:].rearrange("p c d -> p (c d)"), self.banks(6), ACT.Copy).then_inc(self.kd_ready, 1)
        elif kind == "aq":
            h, j = a
            n = self.NC * (P - j * GLA_SUB)
            act.wait_ge(self.argq, h * self.NSUB + j + 1)
            act.activation(self.qt[:, 0:n], self.qt[:, 0:n], ACT.Exp).then_inc(self.eqt, 1)
        elif kind == "sq":
            h, = a
            for d in range(2):
                act.wait_ge(self.o_psum, 2 * h + 2)
                act.wait_ge(self.kd_psum, h + 1)
                act.activation(self.e[d][:], self.banks(4 + 2 * d), ACT.Square).then_inc(self.osq, 1)
        elif kind == "on":
            h, = a
            for c in range(2):
                half = slice(c * HALF, (c + 1) * HALF)
                self.ors.act(act, 2 * h + c, self.e[1][:, half], self.kt[:, half])
        elif kind == "y":
            h, d = a
            n = 2 * h + d
            src = (self.qe, self.b)[d]
            act.wait_ge(self.yt_ready, n + 1)
            act.activation(self.y_hi[:, n, :], src[:], ACT.Copy).then_inc(self.yh_ready, 1)

    def pool(self, pool, kind, *a):
        L = self.L
        if kind == "start":
            pool.memset(self.ident[:], 1.0).then_inc(self.consts, 1)
            pool.memset(self.tri[:], -1.0 / GLA_NORMALIZER).then_inc(self.consts, 1)
            pool.memset(self.mask[:], 1.0).then_inc(self.consts, 1)
            pool.memset(self.a_low, 1.0)
            pool.memset(self.at[:], 0.0)
            pool.wait_ge(self.consts, 3)
            pool.affine_select(out=self.ident[:], in_=self.ident[:], compare_op=ALU.is_equal, fill=0.0, base=0,
                               pattern=[[-1, P]], channel_multiplier=1).then_inc(self.consts, 1)
            pool.affine_select(out=self.tri[:], in_=self.tri[:], compare_op=ALU.is_ge, fill=0.0, base=0,
                               pattern=[[1, P]], channel_multiplier=-1).then_inc(self.consts, 1)
            pool.affine_select(out=self.mask[:], in_=self.mask[:], compare_op=ALU.is_ge, fill=0.0, base=0,
                               pattern=[[1, P]], channel_multiplier=-1).then_inc(self.consts, 2)
            self.norm.pool(pool)
        elif kind == "u":
            if L.units[a[0]][0] == "x":
                self.resid.pool(pool, a[0])
        elif kind == "eq":
            h, = a
            pool.wait_ge(self.eq, h + 1)
            for c in range(2):
                L.wait_unit(pool, self.unit["q", h, c])
            if h:
                pool.wait_ge(self.yl_ready, 2 * h)
            pool.tensor_tensor(self.qe[:], self.q[:], self.e[1][:], ALU.mult).then_inc(self.qe_ready, 1)

    def sync(self, sp, kind, *a):
        L = self.L
        if kind == "start":
            gain_row, head_gain = self.rows
            sp.dma_start(self.gain[:], gain_row).then_inc(self.gain_in, 16)
            sp.dma_start(self.hgain[:], head_gain).then_inc(self.gain_in, 16)
            sp.dma_start(self.wg2[0:GLA_RANK, :], self.w["gate2"]).then_inc(self.gain_in, 16)
            sp.dma_start(self.wg2[GLA_RANK:GLA_RANK + 1, :], self.w["b_gate"]).then_inc(self.gain_in, 16)
        elif kind == "w":
            L.sync_w(sp, *a)


class Net:

    def __init__(self, nc, ctx):
        def sb(name, shape, dt):
            return ctx.enter_context(nc.sbuf_tensor(name, shape, dt))
        self.nc = nc
        self.xT = sb("xT", [P, KD, T], F32)
        self.h_hi, self.h_lo = sb("h_hi", [P, KD, T], F16), sb("h_lo", [P, KD, T], F16)
        self.ssum, self.ones = sb("ssum", [P, T], F32), sb("ones", [P, P], F32)
        self.psum = ctx.enter_context(nc.psum_tensor("psum", [P, 8, HALF], F32))


def load_stream(nc, net, x_in):
    with ExitStack() as ctx:
        x_loaded = [ctx.enter_context(nc.semaphore(f"x_loaded{k}")) for k in range(KD)]
        ones_set = ctx.enter_context(nc.semaphore("ones_set"))
        sq_ready = ctx.enter_context(nc.semaphore("sq0_ready"))
        sum_ready = ctx.enter_context(nc.semaphore("sum0_ready"))
        sq = ctx.enter_context(nc.sbuf_tensor("sq0", [P, 2, T], F32))
        with nc.Block() as block:
            @block.sync
            def _(sp):
                for k in range(KD):
                    sp.dma_start(net.xT[:, k, :], x_in[k * P:(k + 1) * P, :]).then_inc(x_loaded[k], 16)

            @block.gpsimd
            def _(pool):
                pool.memset(net.ones[:], 1.0).then_inc(ones_set, 1)

            @block.scalar
            def _(act):
                act.add_instruction(mybir.InstLoadActFuncSet(
                    name=nc.get_next_instruction_name(), act_func_set_id=EXP_LN_TABLE))
                for k in range(KD):
                    act.wait_ge(x_loaded[k], 16)
                    if k >= 3:
                        act.wait_ge(sum_ready, k - 2)
                    out = net.ssum[:] if k == 0 else sq[:, k % 2, :]
                    act.activation(out, net.xT[:, k, :], ACT.Square).then_inc(sq_ready, 1)

            @block.vector
            def _(dve):
                for k in range(1, KD):
                    dve.wait_ge(sq_ready, k + 1)
                    if k >= 2:
                        dve.wait_ge(sum_ready, k - 1)
                    dve.tensor_tensor(net.ssum[:], net.ssum[:], sq[:, k % 2, :], ALU.add).then_inc(sum_ready, 1)
        clear_semaphores(nc, [*x_loaded, ones_set, sq_ready, sum_ready])


def store_result(nc, net, gain_row, out, stored):
    with ExitStack() as ctx:
        def sem(name):
            return ctx.enter_context(nc.semaphore(f"final_{name}"))
        gain = ctx.enter_context(nc.sbuf_tensor("final_gain", [P, KD], F32))
        m = ctx.enter_context(nc.sbuf_tensor("final_m", [P, T], F32))
        r = ctx.enter_context(nc.sbuf_tensor("final_r", [P, T], F32))
        y = ctx.enter_context(nc.sbuf_tensor("final_y", [P, KD, T], F32))
        gain_in, total, y_ready = sem("gain_in"), sem("total"), sem("y_ready")

        class Tag:
            def sem(self, name):
                return sem(name)
        rsqrt = Rsqrt(Tag(), "rsqrt")
        half = [slice(c * HALF, (c + 1) * HALF) for c in range(2)]
        with nc.Block() as block:
            @block.sync
            def _(sp):
                sp.dma_start(gain[:], gain_row).then_inc(gain_in, 16)
                for c in range(2):
                    for k in range(KD):
                        sp.wait_ge(y_ready, c * KD + k + 1)
                        sp.dma_start(out[k * P:(k + 1) * P, half[c]], y[:, k, half[c]]).then_inc(stored, 16)
                sp.wait_ge(stored, 16 * 2 * KD)

            @block.tensor
            def _(pe):
                for c in range(2):
                    pe.matmul(net.psum[:, c, :], net.ones[:], net.ssum[:, half[c]], start=True,
                              stop=True).then_inc(total, 1)

            @block.scalar
            def _(act):
                for c in range(2):
                    rsqrt.act(act, c, m[:, half[c]], r[:, half[c]])

            @block.vector
            def _(dve):
                dve.wait_ge(gain_in, 16)
                for c in range(2):
                    dve.wait_ge(total, c + 1)
                    rsqrt.dve_m(dve, m[:, half[c]], net.psum[:, c, :], 1.0 / D)
                for c in range(2):
                    rsqrt.dve_newton(dve, c, m[:, half[c]], r[:, half[c]])
                    rsqrt.wait_done(dve, c)
                    for k in range(KD):
                        dve.scalar_tensor_tensor(out=y[:, k, half[c]], in0=net.xT[:, k, half[c]],
                                                 scalar=gain[:, k:k + 1], in1=r[:, half[c]],
                                                 op0=ALU.mult, op1=ALU.mult).then_inc(y_ready, 1)


GLA_PARTS = ("q", "k", "v", "g", "a_low", "gate2", "b_gate", "out")
MLA_PARTS = ("latent", "gate", "up", "q_rope", "out")


def build_trunk(nc, t):
    with ExitStack() as ctx:
        stored = ctx.enter_context(nc.semaphore("result_stored"))
        net = Net(nc, ctx)
        load_stream(nc, net, t["x_T"])
        GatedLinear(nc, net, "gla0", {p: t[f"gla0_{p}"] for p in GLA_PARTS}, t["norm_g0"], t["gla0_head_g"])
        LatentAttention(nc, net, "mla", {p: t[f"mla_{p}"] for p in MLA_PARTS}, t["norm_g1"], t["mla_q_g"],
                        t["mla_kv_g"], t["mla_rope"])
        StickBreaking(nc, net, "sb", t["sb_in"], t["sb_out"], t["norm_g2"])
        GatedLinear(nc, net, "gla1", {p: t[f"gla1_{p}"] for p in GLA_PARTS}, t["norm_g3"], t["gla1_head_g"])
        store_result(nc, net, t["final_g"], t["out_T"], stored)



def column_blocks(w, cols=128):
    import numpy as np
    k, n = w.shape
    w = w.reshape(k // 128, 128, n // cols, cols).transpose(2, 1, 0, 3)
    return np.ascontiguousarray(w.reshape(n // cols, 128, -1))


def gain_columns(v):
    import numpy as np
    return np.ascontiguousarray(v.reshape(-1, 128).T)


def exchange_halves(w):
    k, n = w.shape
    return w.reshape(k, n // MLA_ROPE, 2, MLA_ROPE // 2)[:, :, ::-1, :].reshape(k, n)


def rope_constants():
    import numpy as np
    pos = np.arange(T, dtype=np.float32)
    inv = np.float32(10000.0) ** (-np.arange(0, MLA_ROPE, 2, dtype=np.float32) / np.float32(MLA_ROPE))
    angle = (pos[:, None] * inv[None, :]).T
    c, s = np.cos(angle), np.sin(angle)
    return np.ascontiguousarray(np.stack([np.concatenate([c, c, c, c]), np.concatenate([-s, s, -s, s])]),
                                dtype=np.float32)


def lay_out(inputs):
    import numpy as np
    a = {k: np.asarray(v) for k, v in inputs.items()}
    t = {"x_T": np.ascontiguousarray(a["x"][0].T), "final_g": gain_columns(a["final_g"])}
    for i in range(4):
        t[f"norm_g{i}"] = gain_columns(a["norm_g"][i])
    kd, vd = GLA_HEADS * GLA_DK, GLA_HEADS * GLA_DV
    for i in range(2):
        q, k, v, g, low = np.split(a["gla_w_in"][i], [kd, 2 * kd, 2 * kd + vd, 2 * kd + 2 * vd], axis=1)
        t[f"gla{i}_q"], t[f"gla{i}_k"] = column_blocks(q), column_blocks(k)
        t[f"gla{i}_v"], t[f"gla{i}_g"] = column_blocks(v), column_blocks(g)
        t[f"gla{i}_a_low"] = column_blocks(low, GLA_RANK)[0]
        t[f"gla{i}_gate2"] = a["gla_w_gate2"][i]
        t[f"gla{i}_b_gate"] = a["gla_b_gate"][i][None, :]
        t[f"gla{i}_out"] = column_blocks(a["gla_w_out"][i])
        t[f"gla{i}_head_g"] = gain_columns(a["gla_norm_g"][i])
    cq, ckv, kr, g = np.split(a["mla_w_in"][0], [MLA_QR, MLA_QR + MLA_KVR, MLA_QR + MLA_KVR + MLA_ROPE], axis=1)
    kx = exchange_halves(kr)
    t["mla_latent"] = np.concatenate([column_blocks(cq), column_blocks(ckv),
                                      column_blocks(np.concatenate([kr, kr], axis=1)),
                                      column_blocks(np.concatenate([kx, kx], axis=1))])
    t["mla_gate"] = column_blocks(g)
    uq = a["mla_w_uq"][0].reshape(MLA_QR, MLA_HEADS, MLA_NOPE + MLA_ROPE)
    nope = uq[:, :, :MLA_NOPE].reshape(MLA_QR, -1)
    rope = uq[:, :, MLA_NOPE:].reshape(MLA_QR, -1)
    ukv = a["mla_w_ukv"][0].reshape(MLA_KVR, MLA_HEADS, MLA_NOPE + MLA_V).transpose(1, 0, 2)
    t["mla_up"] = np.concatenate([column_blocks(nope), ukv], axis=2)
    t["mla_q_rope"] = np.concatenate([column_blocks(rope), column_blocks(exchange_halves(rope))], axis=2)
    rows = LatentAttention.GROUP * MLA_V
    t["mla_out"] = np.concatenate([column_blocks(a["mla_w_out"][0][r:r + rows], 256)
                                   for r in range(0, MLA_HEADS * MLA_V, rows)])
    t["mla_q_g"], t["mla_kv_g"] = gain_columns(a["mla_q_norm_g"][0]), gain_columns(a["mla_kv_norm_g"][0])
    t["mla_rope"] = rope_constants()
    t["sb_in"], t["sb_out"] = column_blocks(a["sb_w_in"][0]), column_blocks(a["sb_w_out"][0])
    return {k: np.ascontiguousarray(v) for k, v in t.items()}


def kernel(**inputs):
    import numpy as np
    import concourse.bacc as bacc
    from concourse.bass_utils import run_bass_kernel_spmd

    arrays = lay_out(inputs)
    nc = bacc.Bacc("TRN2", target_bir_lowering=False, num_devices=1)
    tensors = {name: nc.dram_tensor(f"in_{name}", a.shape, mybir.dt.from_np(a.dtype), kind="ExternalInput").ap()
               for name, a in arrays.items()}
    tensors["out_T"] = nc.dram_tensor("out_T", (D, T), F32, kind="ExternalOutput").ap()
    build_trunk(nc, tensors)
    result = run_bass_kernel_spmd(nc, [{f"in_{k}": v for k, v in arrays.items()}], core_ids=[0]).results[0]["out_T"]
    return np.ascontiguousarray(result.T)[None]
```
